# Optimizing a Trainium2 kernel written in Bass

```python
import jax
import jax.numpy as jnp
from jax import lax
import numpy as np

D_MODEL = 1024
BATCH = 1
SEQ = 256
DEPTH = 2

HEAD_DIM = 64
HEADS_PER_MIXER = 4
N_MIXERS = 4
N_HEADS = N_MIXERS * HEADS_PER_MIXER
MIX_WIDTH = N_HEADS * HEAD_DIM
QKV_WIDTH = 3 * HEADS_PER_MIXER * HEAD_DIM
Q_BLOCK = 128
IDX_HEADS = 8
IDX_DIM = 64
DSA_TOPK = 256
DILATED_PAIRS = ((128, 1), (512, 4), (2048, 16))
MOBA_BLOCK = 256
MOBA_TOPK = 3
N_ALIBI_MIXERS = 3
N_ALIBI_HEADS = N_ALIBI_MIXERS * HEADS_PER_MIXER
ALIBI_MAX_EXP = 8.0
N_IN = N_MIXERS * QKV_WIDTH + IDX_HEADS * IDX_DIM + IDX_DIM + IDX_HEADS
D_FF = 2816
N_EXPERTS = 8
TOP_K_EXPERTS = 2
D_FF_EXPERT = 3584
EXPERT_BLOCK = 128
NORM_EPS = 1e-6
ADA_INIT_SCALE = 0.5

kernel_name = "hybrid_sb_dsa_dilated_moba_moe_block"

def _rmsnorm(x, g):
    xf = x.astype(jnp.float32)
    y = xf * lax.rsqrt(jnp.mean(xf * xf, axis=-1, keepdims=True) + NORM_EPS)
    return (y * g.astype(jnp.float32)).astype(x.dtype)

def _alibi_slopes(mixer_pos):
    idx = jnp.arange(HEADS_PER_MIXER, dtype=jnp.float32) * N_ALIBI_MIXERS + (mixer_pos + 1)
    return jnp.exp2(-ALIBI_MAX_EXP * idx / N_ALIBI_HEADS)

def _split_heads(p):
    b, l, _ = p.shape
    p = p.reshape(b, l, 3, HEADS_PER_MIXER, HEAD_DIM)
    return p[:, :, 0].transpose(0, 2, 1, 3), p[:, :, 1].transpose(0, 2, 1, 3), p[:, :, 2].transpose(0, 2, 1, 3)

def _qblock(a, i, axis):
    return lax.dynamic_slice_in_dim(a, i * Q_BLOCK, Q_BLOCK, axis=axis)

def _merge_blocks(out):
    nq, b, h, q, d = out.shape
    return out.transpose(1, 2, 0, 3, 4).reshape(b, h, nq * q, d)

def _stick_breaking_attention(q, k, v):
    b, h, l, dh = q.shape
    scale = dh ** -0.5
    kpos = jnp.arange(l)

    def block(i):
        qs = _qblock(q, i, 2)
        qpos = i * Q_BLOCK + jnp.arange(Q_BLOCK)
        z = jnp.einsum('bhqd,bhkd->bhqk', qs, k).astype(jnp.float32) * scale
        past = kpos[None, :] < qpos[:, None]
        log_1m = jnp.where(past, jax.nn.log_sigmoid(-z), 0.0)
        after = lax.cumsum(log_1m, axis=3, reverse=True) - log_1m
        a = jnp.where(past, jnp.exp(jax.nn.log_sigmoid(z) + after), 0.0)
        return jnp.einsum('bhqk,bhkd->bhqd', a.astype(v.dtype), v)

    return _merge_blocks(lax.map(block, jnp.arange(l // Q_BLOCK)))

def _dsa_attention(q, k, v, q_idx, k_idx, w_idx, slopes):
    b, h, l, dh = q.shape
    n_sel = min(DSA_TOPK, l // 4)
    scale = dh ** -0.5
    kpos = jnp.arange(l)

    def block(i):
        qs = _qblock(q, i, 2)
        qi = _qblock(q_idx, i, 1)
        wi = _qblock(w_idx, i, 1).astype(jnp.float32) * IDX_HEADS ** -0.5
        qpos = i * Q_BLOCK + jnp.arange(Q_BLOCK)
        rel = jax.nn.relu(jnp.einsum('bqhd,bkd->bqhk', qi, k_idx).astype(jnp.float32) * IDX_DIM ** -0.5)
        score = jnp.einsum('bqh,bqhk->bqk', wi, rel)
        score = jnp.where(kpos[None, None, :] <= qpos[None, :, None], score, -jnp.inf)
        sel_score, sel_idx = lax.top_k(score, n_sel)
        kg = jax.vmap(lambda kk, ii: kk[:, ii])(k, sel_idx)
        vg = jax.vmap(lambda vv, ii: vv[:, ii])(v, sel_idx)
        dist = (qpos[None, :, None] - sel_idx).astype(jnp.float32)
        s = jnp.einsum('bhqd,bhqsd->bhqs', qs, kg).astype(jnp.float32) * scale
        s = s - slopes[None, :, None, None] * dist[:, None]
        s = jnp.where(jnp.isfinite(sel_score)[:, None], s, -jnp.inf)
        p = jax.nn.softmax(s, axis=-1)
        return jnp.einsum('bhqs,bhqsd->bhqd', p.astype(v.dtype), vg)

    return _merge_blocks(lax.map(block, jnp.arange(l // Q_BLOCK)))

def _dilated_attention(q, k, v, slopes):
    b, h, l, dh = q.shape
    scale = dh ** -0.5

    def block(i):
        qs = _qblock(q, i, 2)
        qpos = i * Q_BLOCK + jnp.arange(Q_BLOCK)
        outs, lses = [], []
        for window, dilation in DILATED_PAIRS:
            dist = jnp.arange(window // dilation + 1) * dilation
            kpos = qpos[:, None] - dist[None, :]
            kidx = jnp.maximum(kpos, 0)
            kg = k[:, :, kidx]
            vg = v[:, :, kidx]
            s = jnp.einsum('bhqd,bhqnd->bhqn', qs, kg).astype(jnp.float32) * scale
            s = s - slopes[:, None, None] * dist.astype(jnp.float32)
            s = jnp.where(kpos >= 0, s, -jnp.inf)
            m = jnp.max(s, axis=-1, keepdims=True)
            e = jnp.exp(s - m)
            den = jnp.sum(e, axis=-1, keepdims=True)
            outs.append(jnp.einsum('bhqn,bhqnd->bhqd', e, vg.astype(jnp.float32)) / den)
            lses.append(m + jnp.log(den))
        wts = jax.nn.softmax(jnp.stack(lses), axis=0)
        return jnp.sum(wts * jnp.stack(outs), axis=0).astype(v.dtype)

    return _merge_blocks(lax.map(block, jnp.arange(l // Q_BLOCK)))

def _moba_attention(q, k, v, slopes):
    b, h, l, dh = q.shape
    scale = dh ** -0.5
    nb = -(-l // MOBA_BLOCK)
    pad = nb * MOBA_BLOCK - l
    kb = jnp.pad(k, ((0, 0), (0, 0), (0, pad), (0, 0))).reshape(b, h, nb, MOBA_BLOCK, dh)
    vb = jnp.pad(v, ((0, 0), (0, 0), (0, pad), (0, 0))).reshape(b, h, nb, MOBA_BLOCK, dh)
    blk_len = jnp.clip(l - jnp.arange(nb) * MOBA_BLOCK, 1, MOBA_BLOCK).astype(jnp.float32)
    k_mean = kb.astype(jnp.float32).sum(axis=3) / blk_len[:, None]
    n_slots = min(MOBA_TOPK, nb - 1)
    offs = jnp.arange(MOBA_BLOCK)
    gather = jax.vmap(jax.vmap(lambda t, ii: t[ii]))

    def block(i):
        qs = _qblock(q, i, 2)
        qpos = i * Q_BLOCK + jnp.arange(Q_BLOCK)
        own = (i * Q_BLOCK) // MOBA_BLOCK
        k_own = lax.dynamic_index_in_dim(kb, own, axis=2, keepdims=False)
        v_own = lax.dynamic_index_in_dim(vb, own, axis=2, keepdims=False)
        own_pos = own * MOBA_BLOCK + offs
        s_own = jnp.einsum('bhqd,bhxd->bhqx', qs, k_own).astype(jnp.float32) * scale
        s_own = s_own - slopes[:, None, None] * (qpos[:, None] - own_pos[None, :]).astype(jnp.float32)
        s_own = jnp.where(own_pos[None, :] <= qpos[:, None], s_own, -jnp.inf)
        scores = [s_own]
        sel = []
        if n_slots > 0:
            g = jnp.einsum('bhqd,bhnd->bhqn', qs.astype(jnp.float32), k_mean)
            g = jnp.where(jnp.arange(nb) < own, g, -jnp.inf)
            g_val, g_idx = lax.top_k(g, n_slots)
            for j in range(n_slots):
                bj = g_idx[..., j]
                sel.append(bj)
                kg = gather(kb, bj)
                pos = bj[..., None] * MOBA_BLOCK + offs
                s = jnp.einsum('bhqd,bhqxd->bhqx', qs, kg).astype(jnp.float32) * scale
                s = s - slopes[:, None, None] * (qpos[:, None] - pos).astype(jnp.float32)
                s = jnp.where(jnp.isfinite(g_val[..., j:j + 1]), s, -jnp.inf)
                scores.append(s)
        p = jax.nn.softmax(jnp.concatenate(scores, axis=-1), axis=-1).astype(v.dtype)
        out = jnp.einsum('bhqx,bhxd->bhqd', p[..., :MOBA_BLOCK], v_own)
        for j, bj in enumerate(sel):
            vg = gather(vb, bj)
            out = out + jnp.einsum('bhqx,bhqxd->bhqd', p[..., (j + 1) * MOBA_BLOCK:(j + 2) * MOBA_BLOCK], vg)
        return out

    return _merge_blocks(lax.map(block, jnp.arange(l // Q_BLOCK)))

def _token_mixer(h, w_in, g_heads, w_out):
    b, l, _ = h.shape
    p = h @ w_in
    cuts = [int(c) for c in np.cumsum([QKV_WIDTH] * N_MIXERS + [IDX_HEADS * IDX_DIM, IDX_DIM])]
    pa, pb, pc, pd, pqi, pki, pwi = jnp.split(p, cuts, axis=-1)
    o_a = _stick_breaking_attention(*_split_heads(pa))
    o_b = _dsa_attention(*_split_heads(pb), pqi.reshape(b, l, IDX_HEADS, IDX_DIM), pki, pwi, _alibi_slopes(0))
    o_c = _dilated_attention(*_split_heads(pc), _alibi_slopes(1))
    o_d = _moba_attention(*_split_heads(pd), _alibi_slopes(2))
    o = jnp.concatenate([o_a, o_b, o_c, o_d], axis=1)
    o = _rmsnorm(o, g_heads[None, :, None, :])
    o = o.transpose(0, 2, 1, 3).reshape(b, l, MIX_WIDTH)
    return o @ w_out

def _swiglu(h, wg, wu, wd):
    return (jax.nn.silu(h @ wg) * (h @ wu)) @ wd

def _moe_ffn(h, w_router, w_gate, w_up, w_down):
    t, d = h.shape
    logits = h.astype(jnp.float32) @ w_router.astype(jnp.float32)
    top_val, top_idx = lax.top_k(logits, TOP_K_EXPERTS)
    gate = jax.nn.softmax(top_val, axis=-1)
    n_assign = t * TOP_K_EXPERTS
    flat_e = top_idx.reshape(-1).astype(jnp.int32)
    flat_tok = jnp.arange(n_assign, dtype=jnp.int32) // TOP_K_EXPERTS
    flat_g = gate.reshape(-1)
    order = jnp.argsort(flat_e)
    e_s, tok_s, g_s = flat_e[order], flat_tok[order], flat_g[order]
    counts = jnp.bincount(flat_e, length=N_EXPERTS).astype(jnp.int32)
    padded = (counts + EXPERT_BLOCK - 1) // EXPERT_BLOCK * EXPERT_BLOCK
    pad_end = jnp.cumsum(padded)
    pad_start = pad_end - padded
    start = jnp.cumsum(counts) - counts
    dest = pad_start[e_s] + jnp.arange(n_assign, dtype=jnp.int32) - start[e_s]
    n_slots = -(-n_assign // EXPERT_BLOCK) * EXPERT_BLOCK + N_EXPERTS * EXPERT_BLOCK
    n_blocks = n_slots // EXPERT_BLOCK
    slot_tok = jnp.zeros((n_slots,), jnp.int32).at[dest].set(tok_s)
    block_e = jnp.minimum(jnp.searchsorted(pad_end, jnp.arange(n_blocks, dtype=jnp.int32) * EXPERT_BLOCK, side='right'), N_EXPERTS - 1)
    xs = h[slot_tok].reshape(n_blocks, EXPERT_BLOCK, d)

    def expert_block(args):
        xb, e = args
        return _swiglu(xb, w_gate[e], w_up[e], w_down[e])

    ys = lax.map(expert_block, (xs, block_e)).reshape(n_slots, d)
    y_assign = ys[dest] * g_s[:, None].astype(h.dtype)
    return jnp.zeros_like(h).at[tok_s].add(y_assign)

def setup_inputs(seed: int = 0) -> dict:
    key = jax.random.key(seed)
    ks = jax.random.split(key, 17)
    n_dense = (DEPTH + 1) // 2
    n_moe = DEPTH // 2
    f32 = jnp.float32

    def nrm(k, shape, fan_in):
        return jax.random.normal(k, shape, f32) * fan_in ** -0.5

    def gain(k, shape):
        return 1.0 + 0.02 * jax.random.normal(k, shape, f32)

    return {
        'x': jax.random.normal(ks[0], (BATCH, SEQ, D_MODEL), f32),
        'c': jax.random.normal(ks[1], (BATCH, D_MODEL), f32),
        'w_ada': nrm(ks[2], (DEPTH, D_MODEL, 6 * D_MODEL), D_MODEL) * ADA_INIT_SCALE,
        'b_ada': 0.02 * jax.random.normal(ks[3], (DEPTH, 6 * D_MODEL), f32),
        'g_mix': gain(ks[4], (DEPTH, D_MODEL)),
        'w_in': nrm(ks[5], (DEPTH, D_MODEL, N_IN), D_MODEL),
        'g_heads': gain(ks[6], (DEPTH, N_HEADS, HEAD_DIM)),
        'w_out': nrm(ks[7], (DEPTH, MIX_WIDTH, D_MODEL), MIX_WIDTH),
        'g_ffn': gain(ks[8], (DEPTH, D_MODEL)),
        'w_ff_gate': nrm(ks[9], (n_dense, D_MODEL, D_FF), D_MODEL),
        'w_ff_up': nrm(ks[10], (n_dense, D_MODEL, D_FF), D_MODEL),
        'w_ff_down': nrm(ks[11], (n_dense, D_FF, D_MODEL), D_FF),
        'w_router': nrm(ks[12], (n_moe, D_MODEL, N_EXPERTS), D_MODEL),
        'w_exp_gate': nrm(ks[13], (n_moe, N_EXPERTS, D_MODEL, D_FF_EXPERT), D_MODEL),
        'w_exp_up': nrm(ks[14], (n_moe, N_EXPERTS, D_MODEL, D_FF_EXPERT), D_MODEL),
        'w_exp_down': nrm(ks[15], (n_moe, N_EXPERTS, D_FF_EXPERT, D_MODEL), D_FF_EXPERT),
        'g_final': gain(ks[16], (D_MODEL,)),
    }

def reference(x, c, w_ada, b_ada, g_mix, w_in, g_heads, w_out, g_ffn, w_ff_gate, w_ff_up, w_ff_down, w_router, w_exp_gate, w_exp_up, w_exp_down, g_final):
    b, l, d = x.shape
    cond = jax.nn.silu(c)
    for layer in range(DEPTH):
        mod = (cond @ w_ada[layer] + b_ada[layer])[:, None, :]
        shift_m, scale_m, gate_m, shift_f, scale_f, gate_f = jnp.split(mod, 6, axis=-1)
        hm = _rmsnorm(x, g_mix[layer]) * (1 + scale_m) + shift_m
        x = x + gate_m * _token_mixer(hm, w_in[layer], g_heads[layer], w_out[layer])
        hf = _rmsnorm(x, g_ffn[layer]) * (1 + scale_f) + shift_f
        i = layer // 2
        if layer % 2 == 0:
            y = _swiglu(hf, w_ff_gate[i], w_ff_up[i], w_ff_down[i])
        else:
            y = _moe_ffn(hf.reshape(b * l, d), w_router[i], w_exp_gate[i], w_exp_up[i], w_exp_down[i]).reshape(b, l, d)
        x = x + gate_f * y
    return _rmsnorm(x, g_final)


_drawn_inputs = setup_inputs


def setup_inputs(seed=0):
    import zlib

    import numpy as np

    out = dict(_drawn_inputs(seed))
    spreads = {}
    factors = {'g_heads': 3.708, 'g_ffn': 3.318, 'g_final': 2.875}
    for name, (base, spread) in spreads.items():
        noise = np.random.default_rng([zlib.crc32(name.encode()), seed]).standard_normal(out[name].shape)
        drawn = base * np.exp(spread * noise) if base else spread * noise
        out[name] = jnp.asarray(drawn.astype(out[name].dtype))
    for name, factor in factors.items():
        out[name] = (out[name] * factor).astype(out[name].dtype)
    return out
```

```python
from contextlib import ExitStack

import numpy as np

import concourse.bass as bass
from concourse import mybir

F32 = mybir.dt.float32
I32 = mybir.dt.int32
U32 = mybir.dt.uint32
ALU = mybir.AluOpType
ACT = mybir.ActivationFunctionType
AX_X = mybir.AxisListType.X

P = 128
T = 256
D = 1024
KC = D // P
DEPTH = 2
HD = 64
NH = 4
MIX = 4
QKV = 3 * NH * HD
IH = 8
DSA_K = T // 4
FF = 2816
NE = 8
FE = 3584
EXTRA = 3
NR_MAX = NE + EXTRA
EPS = 1e-6
CW = 512
SLOTS = 7
FJ = -(-FF // CW)
EJ = FE // CW
BIG = 1e30
ARENA = 8800
TAKEN = -3e38
SQ = P + T
ALIBI = 12

C_IDENT, C_TRIU, C_NEGTRI, C_NEGONES, C_ONES, C_SLOT = (i * P for i in range(6))
C_STICK = 6 * P
C_CAUSAL = C_STICK + SQ
C_IOTA = C_CAUSAL + SQ
C_DESC = C_IOTA + NE
C_END = C_DESC + NE

ADA = 6 * D // CW
GATES = (4, 5, 10, 11)


def stream():
    out = [("ada", 0, i) for i in range(4)]
    for l in range(DEPTH):
        late = [("ada", 0, i) for i in range(4, ADA)] if l == 0 else [("ada", 1, i) for i in (10, 11)]
        out.append(("idxq", l, 0))
        out += [late.pop(0) for _ in range(min(2, len(late)))]
        out.append(("idxkw", l, 0))
        for m in range(MIX):
            out += [("qk", l, m), ("v", l, m)]
            out += [late.pop(0) for _ in range(min(2, len(late)))]
        out += [("wout", l, 0), ("wout", l, 1)]
        if l == 0:
            for j in range(FJ + 1):
                if j < FJ:
                    out += [("ffg", 0, j), ("ffu", 0, j)]
                if j < 5:
                    out += [("ada", 1, 2 * j), ("ada", 1, 2 * j + 1)]
                if j:
                    out.append(("ffd", 0, j - 1))
    return out


STREAM = stream()
ROUND = [x for j in range(EJ + 2) for x in
         ([("g", j), ("u", j)] if j < EJ else []) + ([("d", j - 2)] if j >= 2 else [])]
PLACE = {key: (i % SLOTS, i // SLOTS) for i, key in enumerate(STREAM)}
BASE = len(STREAM)
PER = len(ROUND) // SLOTS
assert len(ROUND) % SLOTS == 0
RPLACE = {key: ((BASE + i) % SLOTS, (BASE + i) // SLOTS) for i, key in enumerate(ROUND)}


def ada_after(l, at):
    i = STREAM.index(at) + 1
    out = []
    while i < len(STREAM) and STREAM[i][0] == "ada":
        out.append(STREAM[i])
        i += 1
    return out


ADA_ORDER = [k for k in STREAM if k[0] == "ada"]
ADA_NO = {k: n for n, k in enumerate(ADA_ORDER)}


def constants():
    p = np.arange(P)[:, None]
    j = np.arange(P)[None, :]
    ct = np.zeros((P, C_END), np.float32)
    ct[:, C_IDENT:C_IDENT + P] = p == j
    ct[:, C_TRIU:C_TRIU + P] = p <= j
    ct[:, C_NEGTRI:C_NEGTRI + P] = -(p >= j).astype(np.float32)
    ct[:, C_NEGONES:C_NEGONES + P] = -1
    ct[:, C_ONES:C_ONES + P] = 1
    ct[:, C_SLOT:C_SLOT + P] = j + 1
    q = np.arange(T)[None, :]
    ct[:, C_STICK:C_STICK + T] = np.where(p < q, 0, -BIG)
    ct[:, C_STICK + T:C_STICK + SQ] = np.where(p < j, 0, -BIG)
    dist = np.concatenate([p - j, p + P - q], axis=1)
    ct[:, C_CAUSAL:C_CAUSAL + SQ] = np.where(dist >= 0, 0, -BIG)
    ct[:, C_IOTA:C_IOTA + NE] = np.arange(NE)
    ct[:, C_DESC:C_DESC + NE] = NE - np.arange(NE)
    windows = sum(((dist >= 0) & (dist % s == 0) & (dist <= w)).astype(np.float64)
                  for w, s in ((128, 1), (512, 4), (2048, 16)))
    bt = np.zeros((P, ALIBI, SQ), np.float32)
    for mixer in range(3):
        for h in range(NH):
            slope = 2.0 ** (-8.0 * (h * 3 + mixer + 1) / ALIBI)
            seen = windows if mixer == 1 else (dist >= 0).astype(np.float64)
            bt[:, mixer * NH + h] = np.where(seen > 0, slope * dist - np.log(np.maximum(seen, 1)), BIG)
    return ct, bt


def build(nc, x, c, w_ada, b_ada, g_mix, w_in, g_heads, w_out, g_ffn, w_ff_gate, w_ff_up, w_ff_down,
          w_router, w_exp_gate, w_exp_up, w_exp_down, g_final, ctab_in, btab_in, out):
    with ExitStack() as ctx:
        def sb(name, shape, dt=F32):
            return ctx.enter_context(nc.sbuf_tensor(name, shape, dt))

        def sem(name):
            return ctx.enter_context(nc.semaphore(name))

        ring = sb("ring", [P, SLOTS, KC * CW])
        ct = sb("ct", [P, C_END])
        bt = sb("bt", [P, ALIBI, SQ])
        xs = sb("xs", [P, 2, D])
        xn = sb("xn", [P, 2, D])
        hT = sb("hT", [P, KC, T])
        gates = sb("gates", [P, 2, D])
        acc = sb("acc", [P, CW])
        rows = sb("rows", [P, P])
        rows2 = sb("rows2", [24, P])
        cols = sb("cols", [P, 152])
        cond = sb("cond", [P, KC])
        mcol = sb("mcol", [P, DEPTH, 48])
        acol = sb("acol", [P, DEPTH, 2, KC])
        st = sb("st", [P, 64])
        epst = sb("epst", [P, 2])
        arena = sb("arena", [P, ARENA])

        class At:
            at = 0

        def part(n):
            At.at += n
            assert At.at <= ARENA
            return arena[:, At.at - n:At.at]

        qkT = part(2 * 4 * T).rearrange("p (b t n) -> p b t n", b=2, t=4)
        iq = part(4 * T).rearrange("p (t n) -> p t n", t=4)
        vAB = part(2 * 2 * T).rearrange("p (m b n) -> p m b n", m=2, b=2)
        vCD = iq.rearrange("p (m b) n -> p m b n", m=2)
        ik = part(T)
        sc = part(2 * SQ).rearrange("p (b n) -> p b n", b=2)
        selm = part(SQ)
        zb = part(NH * SQ).rearrange("p (h n) -> p h n", h=NH)
        eb = part(NH * SQ).rearrange("p (h n) -> p h n", h=NH)
        relu = zb[:, 0:2]
        nb = eb[:, 0:2]
        ex = eb[:, 2:4]
        pt = zb[:, 0:2]
        iw = part(16).rearrange("p (b h) -> p b h", b=2)
        v8 = part(8)
        mn = part(24).rearrange("p (b h) -> p b h", b=2)
        den = part(24).rearrange("p (b h) -> p b h", b=2)
        rden = part(24).rearrange("p (b h) -> p b h", b=2)
        At.at = 0
        ffT = part(2 * 4 * T).rearrange("p (b t n) -> p b t n", b=2, t=4)
        fsg = part(2 * T).rearrange("p (b n) -> p b n", b=2)
        At.at = 0
        xsT = part(KC * P).rearrange("p (c n) -> p c n", c=KC)
        sg = part(2 * CW).rearrange("p (b n) -> p b n", b=2)
        hs = part(2 * CW).rearrange("p (b n) -> p b n", b=2)
        hsT = part(2 * CW).rearrange("p (b t n) -> p b t n", b=2, t=4)
        ys = part(D)
        yacc = part(2 * D).rearrange("p (b n) -> p b n", b=2)
        sel01 = part(T).rearrange("p (b n) -> p b n", b=2)
        selg = part(T).rearrange("p (b n) -> p b n", b=2)
        selgT = part(T)
        lg = part(2 * NE).rearrange("p (b e) -> p b e", b=2)
        top = part(2 * NE).rearrange("p (b e) -> p b e", b=2)
        topi = sb("topi", [P, 2, 8], U32)
        topf = part(2 * NE).rearrange("p (b e) -> p b e", b=2)
        oh = part(4 * NE).rearrange("p (b k e) -> p b k e", b=2, k=2)
        chosen = part(2 * NE).rearrange("p (b e) -> p b e", b=2)
        gt = part(8).rearrange("p (b e) -> p b e", b=2)
        pos = part(2 * NR_MAX).rearrange("p (b r) -> p b r", b=2)
        gate = part(2 * NR_MAX).rearrange("p (b r) -> p b r", b=2)
        key = part(NE)
        key8 = part(NE)
        over = part(NE)
        roh = part(EXTRA * NE).rearrange("p (r e) -> p r e", r=EXTRA)
        scr = part(NE)
        nxf = part(4)
        wr = part(KC * NE).rearrange("p (c e) -> p c e", c=KC)
        route_i = sb("route_i", [P, 4], I32)
        gfin = bt[:, 0:3, :].rearrange("p a n -> p (a n)")[:, 0:D]

        bank = [ctx.enter_context(nc.psum_tensor(f"bank{i}", [P, CW], F32)) for i in range(8)]

        full = [sem(f"full{i}") for i in range(SLOTS)]
        s_const, s_tab, s_x, s_rows = sem("const_in"), sem("tables_in"), sem("x_in"), sem("rows_in")
        s_wr, s_gfin, s_out = sem("router_in"), sem("gfinal_in"), sem("out_done")
        setup_t, setup_c = sem("setup_transposed"), sem("setup_copied")
        cond_r = sem("cond_ready")
        acc_r, ada_p, ada_c = sem("ada_sums"), sem("ada_product"), sem("ada_copied")
        ss_r, sq_r, xn_r = sem("square_sums"), sem("root"), sem("xn_ready")
        tr_p, tr_v, tr_a = sem("transposed"), sem("transposed_copied_v"), sem("transposed_copied_a")
        proj_p, proj_c = sem("projected"), sem("projected_copied")
        is_p, is_a, is_v = sem("index_scores"), sem("index_relu"), sem("index_sum")
        z_p, z_v, sp_r = sem("stick_scores"), sem("stick_scores_copied"), sem("stick_softplus")
        ze_a = sem("stick_exp_ln")
        suf_p, stT_v, stA_a = sem("stick_suffix"), sem("stick_log_weights"), sem("stick_weights")
        s_p, n_v, e_a = sem("scores"), sem("biased_scores"), sem("exponentials")
        pt_p, pt_c = sem("weights_transposed"), sem("weights_copied")
        o_p, o_v = sem("mixer_output"), sem("mixer_output_copied")
        hr_v, hq_a, on_v = sem("head_square_sums"), sem("head_roots"), sem("heads_normed")
        wo_p, x_v = sem("mixed"), sem("x_updated")
        gu_p, sg_a, h_v, y_p = sem("gate_up"), sem("silu"), sem("hidden"), sem("ffn_out")
        r_p, r_v, r_a, route_v = sem("router_product"), sem("router_step"), sem("router_exp"), sem("routed")
        sel_v, gat_p, xsT_v, xsT_a = sem("one_hots"), sem("gathered"), sem("gathered_v"), sem("gathered_a")
        sgt_p, sgt_v = sem("scatter_transposed"), sem("scatter_matrix")
        egu_p, esg_a, eh_v = sem("expert_gate_up"), sem("expert_silu"), sem("expert_hidden")
        et_p, et_a, ey_p = sem("expert_hidden_t"), sem("expert_hidden_t_copied"), sem("expert_out")
        ys_a, sct_p, yacc_v = sem("expert_out_copied"), sem("scattered"), sem("y_summed")
        dv, fin_a, fin_v = sem("vector_chain"), sem("final_act"), sem("final_ready")

        ident = ct[:, C_IDENT:C_IDENT + P]
        ones = ct[:, C_ONES:C_ONES + P]

        def slot(key, n, place=PLACE):
            return ring[:, place[key][0], 0:KC * n].rearrange("p (c n) -> p c n", c=KC)

        def slot_rows(key, nr, place=PLACE):
            return ring[:, place[key][0], 0:nr * D].rearrange("p (c n) -> p c n", c=nr)

        def arrived(eng, key):
            s, u = PLACE[key]
            eng.wait_ge(full[s], 16 * (u + 1))

        def released(key):
            kind, l, i = key
            return {"ada": (acc_r, ADA_NO.get(key, 0) + 1), "idxq": (proj_p, 25 * l + 4), "idxkw": (proj_p, 25 * l + 5),
                    "qk": (proj_p, 25 * l + 9 + 5 * i), "v": (proj_p, 25 * l + 10 + 5 * i),
                    "wout": (wo_p, 4 * l + 2 * i + 2), "ffg": (gu_p, min(4 * i + 4, FF // P)),
                    "ffu": (gu_p, min(4 * i + 4, FF // P)), "ffd": (y_p, i + 1)}[kind]

        def norm_no(l, which):
            return 3 * l + which

        def ff_tiles(j):
            return (min(FF, (j + 1) * CW) - j * CW) // P

        block = ctx.enter_context(nc.Block())

        @block.sync
        def _(sp):
            def source(key):
                kind, l, i = key
                kview = lambda w, a, b: w[:, a:b].rearrange("(c p) n -> p c n", p=P)
                if kind == "ada":
                    return kview(w_ada[l], i * CW, (i + 1) * CW), slot(key, CW)
                if kind == "idxq":
                    return kview(w_in[l], MIX * QKV, MIX * QKV + CW), slot(key, CW)
                if kind == "idxkw":
                    a = MIX * QKV + CW
                    return kview(w_in[l], a, a + HD + IH), slot(key, HD + IH)
                if kind == "qk":
                    return kview(w_in[l], i * QKV, i * QKV + CW), slot(key, CW)
                if kind == "v":
                    return kview(w_in[l], i * QKV + CW, (i + 1) * QKV), slot(key, T)
                if kind == "wout":
                    return kview(w_out[l], i * CW, (i + 1) * CW), slot(key, CW)
                n = ff_tiles(i)
                if kind == "ffd":
                    return (w_ff_down[0, i * CW:i * CW + n * P, :].rearrange("(c p) n -> p c n", p=P),
                            slot_rows(key, n))
                return kview((w_ff_gate if kind == "ffg" else w_ff_up)[0], i * CW, i * CW + n * P), slot(key, n * P)

            def load(key):
                s, u = PLACE[key]
                n = STREAM.index(key)
                if n >= SLOTS:
                    sp.wait_ge(*released(STREAM[n - SLOTS]))
                src, dst = source(key)
                sp.dma_start(dst, src).then_inc(full[s], 16)

            sp.dma_start(rows[0:96, :], b_ada.rearrange("l (j p) -> (l j) p", p=P)).then_inc(s_rows, 16)
            sp.dma_start(rows[96:112, :], g_mix.rearrange("l (j p) -> (l j) p", p=P)).then_inc(s_rows, 16)
            sp.dma_start(rows[112:128, :], g_ffn.rearrange("l (j p) -> (l j) p", p=P)).then_inc(s_rows, 16)
            sp.dma_start(rows2[0:16, :], g_heads.rearrange("l (j a) d -> (l j) (a d)", a=2)).then_inc(s_rows, 16)
            sp.dma_start(rows2[16:24, :], c.rearrange("a (j p) -> (a j) p", p=P)).then_inc(s_rows, 16)
            sp.dma_start(ct[:, :], ctab_in).then_inc(s_const, 16)
            sp.dma_start(xs[:, :, :], x[0].rearrange("(b p) n -> p b n", p=P)).then_inc(s_x, 16)
            for n, key in enumerate(STREAM):
                load(key)
                if n == 5:
                    sp.dma_start(bt[:, :, :], btab_in).then_inc(s_tab, 16)

            def load_piece(r, expert, i, before):
                what, j = ROUND[i]
                s, u = RPLACE[what, j]
                if before:
                    sp.wait_ge(*released(STREAM[BASE + i - SLOTS]))
                else:
                    old, oj = ROUND[i - SLOTS]
                    last = r if i >= SLOTS else r - 1
                    sp.wait_ge(ey_p if old == "d" else egu_p, last * EJ + oj + 1)
                if what == "d":
                    src = w_exp_down[0, bass.ds(expert, 1), j * CW:(j + 1) * CW, :]
                    dst = slot_rows((what, j), 4, RPLACE)
                else:
                    src = (w_exp_gate if what == "g" else w_exp_up)[0, bass.ds(expert, 1), :, j * CW:(j + 1) * CW]
                    dst = slot((what, j), CW, RPLACE)
                sp.dma_start(dst, src.rearrange("e (c p) n -> p (e c) n", p=P)).then_inc(full[s], 16)

            for i in range(SLOTS):
                load_piece(0, 0, i, True)
            with sp.Fori(0, NE - 1) as r:
                for i in range(SLOTS, len(ROUND)):
                    load_piece(r, r, i, False)
                for i in range(SLOTS):
                    load_piece(r + 1, r + 1, i, False)
            for i in range(SLOTS, len(ROUND)):
                load_piece(NE - 1, NE - 1, i, False)
            sp.wait_ge(n_v, DEPTH * ALIBI)
            sp.dma_start(gfin, g_final.rearrange("(a n) -> a n", a=1).to_broadcast([P, D])).then_inc(s_gfin, 16)
            sp.wait_ge(route_v, 1)
            rounds = sp.value_load(route_i[0:1, 3:4], min_val=NE, max_val=NR_MAX)
            with sp.If(rounds > NE):
                with sp.Fori(NE, rounds) as r:
                    expert = sp.value_load(route_i[0:1, bass.ds(r - NE, 1)], min_val=0, max_val=NE - 1)
                    for i in range(len(ROUND)):
                        load_piece(r, expert, i, False)
            sp.wait_ge(fin_v, 1)
            sp.dma_start(out[0].rearrange("(b p) n -> p b n", p=P), xn[:, :, :]).then_inc(s_out, 16)
            sp.wait_ge(s_out, 16)

        @block.tensor
        def _(pe):
            mm = nc.tensor.matmul

            def ada(key):
                n = ADA_NO[key]
                _, l, i = key
                pe.wait_ge(acc_r, n + 1)
                if n:
                    pe.wait_ge(ada_c, n)
                a = acc[:, :]
                if i in GATES:
                    mm(bank[2][:, :], ones, a, start=True, stop=True)
                    for t in range(4):
                        row = l * 48 + 4 * i + t
                        last = mm(bank[2][:, t * P:(t + 1) * P], ident[:, row:row + 1].to_broadcast([P, P]), rows[:, :],
                                  start=False, stop=True, skip_group_check=True)
                else:
                    for t in range(4):
                        last = mm(bank[2][:, t:t + 1], a[:, t * P:(t + 1) * P], ones[:, 0:1], start=True, stop=True)
                last.then_inc(ada_p, 1)

            def turn(no):
                if no % 3 == 1:
                    pe.wait_ge(on_v, no // 3 + 1)
                else:
                    pe.wait_ge(xn_r, 2 * (no // 3) + (no % 3 == 2) + 1)
                for g in range(4):
                    for cc in range(2):
                        for b in range(2):
                            ch = 2 * g + cc
                            last = nc.tensor.transpose(bank[4 + g][:, cc * T + b * P:cc * T + (b + 1) * P],
                                                       xn[:, b, ch * P:(ch + 1) * P], ident)
                    last.then_inc(tr_p, 1)

            def turned(no):
                pe.wait_ge(tr_v, 4 * (no + 1))
                pe.wait_ge(tr_a, 4 * (no + 1))

            def group(G):
                if G >= 2:
                    pe.wait_ge(proj_c, G - 1)
                return bank[G % 2]

            pe.wait_ge(s_const, 16)
            pe.wait_ge(s_rows, 80)
            nc.tensor.transpose(bank[4][:, 0:P], rows[:, :], ident)
            nc.tensor.transpose(bank[4][:, P:P + 24], rows2[:, :], ident[0:24, 0:24]).then_inc(setup_t, 1)
            for i in range(4):
                ada(("ada", 0, i))

            for l in range(DEPTH):
                def tiles(key, g0, n, w_cols):
                    arrived(pe, key)
                    w = slot(key, w_cols)
                    for t in range(n):
                        G = 25 * l + g0 + t
                        o = group(G)
                        for k in range(KC):
                            last = mm(o[:, 0:T], w[:, k, t * P:(t + 1) * P], hT[:, k, :],
                                      start=(k == 0), stop=(k == KC - 1))
                        last.then_inc(proj_p, 1)

                turn(norm_no(l, 0))
                turned(norm_no(l, 0))
                tiles(("idxq", l, 0), 0, 4, CW)
                for key in ada_after(l, ("idxq", l, 0)):
                    ada(key)
                arrived(pe, ("idxkw", l, 0))
                w = slot(("idxkw", l, 0), HD + IH)
                o = group(25 * l + 4)
                for half in (0, 64):
                    for k in range(KC):
                        mm(o[half:half + HD, 0:T], w[:, k, 0:HD], hT[:, k, :], start=(k == 0), stop=(k == KC - 1))
                for b in range(2):
                    for k in range(KC):
                        last = mm(o[:, T + b * IH:T + (b + 1) * IH], hT[:, k, b * P:(b + 1) * P], w[:, k, HD:HD + IH],
                                  start=(k == 0), stop=(k == KC - 1))
                last.then_inc(proj_p, 1)

                def project(m):
                    tiles(("qk", l, m), 5 + 5 * m, 4, CW)
                    key = ("v", l, m)
                    arrived(pe, key)
                    w = slot(key, T)
                    o = group(25 * l + 9 + 5 * m)
                    for b in range(2):
                        for k in range(KC):
                            last = mm(o[:, b * T:(b + 1) * T], hT[:, k, b * P:(b + 1) * P], w[:, k, :],
                                      start=(k == 0), stop=(k == KC - 1))
                    last.then_inc(proj_p, 1)
                    for k in ada_after(l, key):
                        ada(k)

                def half(h):
                    return slice(HD * (h % 2), HD * (h % 2) + HD)

                def values(m):
                    return vAB[:, m] if m < 2 else vCD[:, m - 2]

                project(0)
                pe.wait_ge(proj_c, 25 * l + 5)
                for h in range(IH):
                    if h >= 4:
                        pe.wait_ge(is_a, IH * l + h - 3)
                    o = bank[4 + h % 4]
                    mm(o[:, 0:P], iq[half(h), h // 2, 0:P], ik[half(h), 0:P], start=True, stop=True)
                    mm(o[:, P:SQ], iq[half(h), h // 2, P:T], ik[half(h), :], start=True, stop=True).then_inc(is_p, 1)
                project(1)
                for h in range(NH):
                    pe.wait_ge(is_a, IH * l + 5 + h)
                    pe.wait_ge(proj_c, 25 * l + 9)
                    q, k = qkT[half(h), 0, h // 2, :], qkT[half(h), 0, 2 + h // 2, :]
                    mm(bank[4 + h][:, 0:T], k[:, 0:P], q, start=True, stop=True)
                    mm(bank[4 + h][:, T:SQ], k[:, P:T], q[:, P:T], start=True, stop=True).then_inc(z_p, 1)
                project(2)
                for h in range(NH):
                    pe.wait_ge(sp_r, NH * l + h + 1)
                    o = bank[4 + h]
                    mm(o[:, 0:T], ct[:, C_NEGTRI:C_NEGTRI + P], eb[:, h, 0:T], start=True, stop=True)
                    mm(o[:, P:T], ct[:, C_NEGONES:C_NEGONES + P], eb[:, h, T:SQ], start=False, stop=True,
                       skip_group_check=True)
                    mm(o[:, T:SQ], ct[:, C_NEGTRI:C_NEGTRI + P], eb[:, h, T:SQ], start=True, stop=True).then_inc(suf_p, 1)

                def pv(m, h, wt, o):
                    v = values(m)
                    mm(o[:, h * HD:(h + 1) * HD], wt[:, 0:P], v[:, 0, h * HD:(h + 1) * HD], start=True, stop=True)
                    dst = o[:, T + h * HD:T + (h + 1) * HD]
                    mm(dst, wt[:, P:T], v[:, 0, h * HD:(h + 1) * HD], start=True, stop=False)
                    return mm(dst, wt[:, T:SQ], v[:, 1, h * HD:(h + 1) * HD], start=False, stop=True)

                def out_bank(m):
                    if 4 * l + m:
                        pe.wait_ge(o_v, 4 * l + m)

                for h in range(NH):
                    pe.wait_ge(stA_a, NH * l + h + 1)
                    if h == 0:
                        out_bank(0)
                    last = pv(0, h, zb[:, h, :], bank[3])
                last.then_inc(o_p, 1)

                def score(n):
                    m, h = 1 + n // NH, n % NH
                    N = ALIBI * l + n
                    pe.wait_ge(proj_c, 25 * l + 9 + 5 * m)
                    if n >= 2:
                        pe.wait_ge(n_v, N - 1)
                    else:
                        pe.wait_ge(stT_v, NH * (l + 1))
                    o = bank[4 + n % 2]
                    q, k = qkT[half(h), m % 2, h // 2, :], qkT[half(h), m % 2, 2 + h // 2, :]
                    mm(o[:, 0:P], q[:, 0:P], k[:, 0:P], start=True, stop=True)
                    mm(o[:, P:SQ], q[:, P:T], k, start=True, stop=True).then_inc(s_p, 1)

                def turn_weights(n):
                    N = ALIBI * l + n
                    pe.wait_ge(e_a, N + 1)
                    if n >= 2:
                        pe.wait_ge(pt_c, N - 1)
                    for t in range(3):
                        last = nc.tensor.transpose(bank[6 + n % 2][:, t * P:(t + 1) * P],
                                                   ex[:, n % 2, t * P:(t + 1) * P], ident)
                    last.then_inc(pt_p, 1)

                def apply(n):
                    m, h = 1 + n // NH, n % NH
                    pe.wait_ge(pt_c, ALIBI * l + n + 1)
                    if h == 0:
                        out_bank(m)
                    pv(m, h, pt[:, n % 2, :], bank[3]).then_inc(o_p, 1)

                def softmax_heads(n0, n1):
                    for n in range(n0, n1 + 2):
                        if n < n1:
                            score(n)
                        if n0 <= n - 1 < n1:
                            turn_weights(n - 1)
                        if n - 2 >= n0:
                            apply(n - 2)

                softmax_heads(0, NH)
                project(3)
                softmax_heads(NH, ALIBI)
                turn(norm_no(l, 1))
                turned(norm_no(l, 1))
                for hf in range(2):
                    key = ("wout", l, hf)
                    arrived(pe, key)
                    w = slot(key, CW)
                    for b in range(2):
                        for k in range(KC):
                            last = mm(bank[4 + 2 * hf + b][:, :], hT[:, k, b * P:(b + 1) * P], w[:, k, :],
                                      start=(k == 0), stop=(k == KC - 1))
                        last.then_inc(wo_p, 1)
                turn(norm_no(l, 2))
                turned(norm_no(l, 2))
                if l == 0:
                    n = 0
                    for j in range(FJ + 1):
                        if j < FJ:
                            arrived(pe, ("ffg", 0, j))
                            arrived(pe, ("ffu", 0, j))
                            w = [slot((kind, 0, j), ff_tiles(j) * P) for kind in ("ffg", "ffu")]
                            for t in range(ff_tiles(j)):
                                if n >= 2:
                                    pe.wait_ge(h_v, n - 1)
                                for a in range(2):
                                    for k in range(KC):
                                        last = mm(bank[n % 2][:, a * T:(a + 1) * T], w[a][:, k, t * P:(t + 1) * P],
                                                  hT[:, k, :], start=(k == 0), stop=(k == KC - 1))
                                last.then_inc(gu_p, 1)
                                n += 1
                        if j < 5:
                            for i in (2 * j, 2 * j + 1):
                                ada(("ada", 1, i))
                        if j:
                            key = ("ffd", 0, j - 1)
                            arrived(pe, key)
                            w = slot_rows(key, ff_tiles(j - 1))
                            pe.wait_ge(h_v, min(4 * j, FF // P))
                            for r in range(ff_tiles(j - 1)):
                                for b in range(2):
                                    for hf in range(2):
                                        last = mm(bank[4 + 2 * hf + b][:, :], ffT[:, (j - 1) % 2, r, b * P:(b + 1) * P],
                                                  w[:, r, hf * CW:(hf + 1) * CW], start=(j == 1 and r == 0),
                                                  stop=(j == FJ and r == ff_tiles(j - 1) - 1))
                            last.then_inc(y_p, 1)

            pe.wait_ge(s_wr, 16)
            for b in range(2):
                for k in range(KC):
                    last = mm(bank[0][:, b * NE:(b + 1) * NE], hT[:, k, b * P:(b + 1) * P], wr[:, k, :],
                              start=(k == 0), stop=(k == KC - 1))
            last.then_inc(r_p, 1)
            pe.wait_ge(sel_v, 1)
            mm(bank[1][:, 0:NE], ct[:, C_TRIU:C_TRIU + P], chosen[:, 0, :], start=True, stop=True)
            mm(bank[1][:, NE:2 * NE], ones, chosen[:, 0, :], start=True, stop=False)
            mm(bank[1][:, NE:2 * NE], ct[:, C_TRIU:C_TRIU + P], chosen[:, 1, :], start=False, stop=True)
            mm(bank[1][:, 2 * NE:3 * NE], ones, chosen[:, 0, :], start=True, stop=False)
            mm(bank[1][:, 2 * NE:3 * NE], ones, chosen[:, 1, :], start=False, stop=True).then_inc(r_p, 1)

            pe.wait_ge(route_v, 1)
            rounds = pe.value_load(route_i[0:1, 3:4], min_val=NE, max_val=NR_MAX)
            with pe.Fori(0, rounds) as r:
                pe.wait_ge(sel_v, r + 2)
                for k in range(KC):
                    for b in range(2):
                        last = mm(bank[4 + k // 4][:, (k % 4) * P:(k % 4 + 1) * P], xn[:, b, k * P:(k + 1) * P],
                                  sel01[:, b, :], start=(b == 0), stop=(b == 1))
                last.then_inc(gat_p, 1)
                for b in range(2):
                    last = nc.tensor.transpose(bank[6][:, b * P:(b + 1) * P], selg[:, b, :], ident)
                last.then_inc(sgt_p, 1)
                pe.wait_ge(xsT_v, 4 * r + 4)
                pe.wait_ge(xsT_a, 4 * r + 4)
                for j in range(EJ + 2):
                    if j < EJ:
                        if j == 0:
                            pe.wait_ge(yacc_v, 4 * r + 1)
                        if j >= 2:
                            pe.wait_ge(eh_v, EJ * r + j - 1)
                        for a, what in enumerate("gu"):
                            s, u = RPLACE[what, j]
                            pe.wait_ge(full[s], r * (16 * PER) + 16 * (u + 1))
                            w = slot((what, j), CW, RPLACE)
                            for k in range(KC):
                                last = mm(bank[2 * (j % 2) + a][:, :], xsT[:, k, :], w[:, k, :],
                                          start=(k == 0), stop=(k == KC - 1))
                        last.then_inc(egu_p, 1)
                    if 1 <= j <= EJ:
                        pe.wait_ge(eh_v, EJ * r + j)
                        if j >= 3:
                            pe.wait_ge(et_a, EJ * r + j - 2)
                        for t in range(4):
                            last = nc.tensor.transpose(bank[4 + (j - 1) % 2][:, t * P:(t + 1) * P],
                                                       hs[:, (j - 1) % 2, t * P:(t + 1) * P], ident)
                        last.then_inc(et_p, 1)
                    if j >= 2:
                        pe.wait_ge(et_a, EJ * r + j - 1)
                        if j == 2:
                            pe.wait_ge(sgt_v, r + 1)
                        s, u = RPLACE["d", j - 2]
                        pe.wait_ge(full[s], r * (16 * PER) + 16 * (u + 1))
                        w = slot_rows(("d", j - 2), 4, RPLACE)
                        for t in range(4):
                            for hf in range(2):
                                last = mm(bank[6 + hf][:, :], hsT[:, (j - 2) % 2, t, :], w[:, t, hf * CW:(hf + 1) * CW],
                                          start=(j == 2 and t == 0), stop=(j == EJ + 1 and t == 3))
                        last.then_inc(ey_p, 1)
                pe.wait_ge(ys_a, r + 1)
                for b in range(2):
                    for hf in range(2):
                        last = mm(bank[2 * hf + b][:, :], selgT[:, b * P:(b + 1) * P], ys[:, hf * CW:(hf + 1) * CW],
                                  start=True, stop=True)
                last.then_inc(sct_p, 1)

        @block.vector
        def _(ve):
            ts, tt, stt = nc.vector.tensor_scalar, nc.vector.tensor_tensor, nc.vector.scalar_tensor_tensor
            ttr = nc.vector.tensor_tensor_reduce
            count = {}

            def signal(ins, s):
                ins.then_inc(s, 1)
                count[s.name] = count.get(s.name, 0) + 1

            def own(s):
                ve.wait_ge(s, count[s.name])

            def then(ins):
                signal(ins, dv)
                own(dv)

            def ada_sum(key):
                n = ADA_NO[key]
                ve.wait_ge(cond_r, 1)
                if n:
                    ve.wait_ge(ada_p, n)
                arrived(ve, key)
                w = slot(key, CW)
                then(ts(acc[:, :], w[:, 0, :], cond[:, 0:1], None, ALU.mult))
                for k in range(1, KC):
                    ins = stt(acc[:, :], w[:, k, :], cond[:, k:k + 1], acc[:, :], ALU.mult, ALU.add)
                    if k < KC - 1:
                        then(ins)
                    else:
                        signal(ins, acc_r)

            def ada_take(key):
                _, l, i = key
                ve.wait_ge(ada_p, ADA_NO[key] + 1)
                if i in GATES:
                    if l:
                        own(x_v)
                    dst = gates[:, GATES.index(i) // 2, (i % 2) * CW:(i % 2 + 1) * CW]
                    signal(nc.vector.tensor_copy(dst, bank[2][:, :]), ada_c)
                    return
                part = mcol[:, l, 4 * i:4 * i + 4]
                ins = tt(part, bank[2][:, 0:4], cols[:, l * 48 + 4 * i:l * 48 + 4 * i + 4], ALU.add)
                if i // 2 in (1, 4):
                    then(ins)
                    w = i // 2 // 4
                    g0 = 96 + 16 * w + 8 * l + 4 * (i % 2)
                    ins = stt(acol[:, l, w, 4 * (i % 2):4 * (i % 2) + 4], part, 1.0, cols[:, g0:g0 + 4],
                              ALU.add, ALU.mult)
                signal(ins, ada_c)

            def ada(keys):
                for key in keys:
                    ada_sum(key)
                    ada_take(key)

            def norm(no):
                ve.wait_ge(sq_r, no + 1)
                then(nc.vector.reciprocal(st[:, 4:6], st[:, 2:4]))
                ts(xn[:, 0, :], xs[:, 0, :], st[:, 4:5], None, ALU.mult)
                signal(ts(xn[:, 1, :], xs[:, 1, :], st[:, 5:6], None, ALU.mult), xn_r)

            def turned(no):
                l, which = no // 3, no % 3
                if which != 1:
                    own(ada_c)
                for k in (0, 1, 4, 5):
                    g = k // 2
                    ve.wait_ge(tr_p, 4 * no + g + 1)
                    src = bank[4 + g][:, (k % 2) * T:(k % 2 + 1) * T]
                    if which == 1:
                        ins = ts(hT[:, k, :], src, cols[:, 128 + 8 * l + k:129 + 8 * l + k], None, ALU.mult)
                    else:
                        w = which // 2
                        ins = ts(hT[:, k, :], src, acol[:, l, w, k:k + 1],
                                 mcol[:, l, 24 * w + k:24 * w + k + 1], ALU.mult, ALU.add)
                    signal(ins, tr_v)

            def add_to_x(kind, hf, b, n):
                tmp = zb.rearrange("p h n -> p (h n)")[:, (n % 2) * CW:(n % 2 + 1) * CW]
                own(ada_c)
                if x_v.name in count:
                    own(x_v)
                then(tt(tmp, bank[4 + 2 * hf + b][:, :], gates[:, kind, hf * CW:(hf + 1) * CW], ALU.mult))
                part = xs[:, b, hf * CW:(hf + 1) * CW]
                signal(tt(part, part, tmp, ALU.add), x_v)

            nc.vector.memset(epst[:, 0:1], EPS)
            signal(nc.vector.memset(epst[:, 1:2], 1.0), dv)
            ve.wait_ge(setup_t, 1)
            signal(nc.vector.tensor_copy(cols[:, :], bank[4][:, 0:P + 24]), setup_c)
            own(setup_c)
            ada([("ada", 0, i) for i in range(4)])

            def heads(l, n0, n1):
                for n in range(n0, n1 + 2):
                    if n < n1:
                        N = ALIBI * l + n
                        ve.wait_ge(s_p, N + 1)
                        if n == 0 and l == 0:
                            ve.wait_ge(s_tab, 16)
                        if n >= 2:
                            ve.wait_ge(e_a, N - 1)
                        s = bank[4 + n % 2][:, 0:SQ]
                        dst = nb[:, n % 2, :]
                        if n < NH:
                            then(tt(dst, s, selm, ALU.add))
                            s = dst
                        ttr(dst[:, 0:P], s[:, 0:P], bt[:, n, 0:P], 1.0, 3e38, ALU.add, ALU.min, mn[:, 0, n:n + 1])
                        signal(ttr(dst[:, P:SQ], s[:, P:SQ], bt[:, n, P:SQ], 1.0, 3e38, ALU.add, ALU.min,
                                   mn[:, 1, n:n + 1]), n_v)
                    if n0 <= n - 1 < n1:
                        N = ALIBI * l + n - 1
                        ve.wait_ge(pt_p, N + 1)
                        if n - 1 >= 2:
                            ve.wait_ge(o_p, 13 * l + 1 + n - 2)
                        signal(nc.vector.tensor_copy(pt[:, (n - 1) % 2, :], bank[6 + (n - 1) % 2][:, 0:SQ]), pt_c)
                    if n - 2 >= n0 and (n - 2) % NH == NH - 1:
                        m = 1 + (n - 2) // NH
                        hh = slice(n - 2 - NH + 1, n - 1)
                        ve.wait_ge(o_p, 13 * l + 1 + n - 1)
                        then(nc.vector.reciprocal(rden[:, :, hh], den[:, :, hh]))
                        dst = xn[:, :, m * T:(m + 1) * T].rearrange("p b (h d) -> p b h d", h=NH)
                        src = bank[3][:, :].rearrange("p (b h d) -> p b h d", b=2, h=NH)
                        signal(tt(dst, src, rden[:, :, hh].unsqueeze(3).to_broadcast([P, 2, NH, HD]), ALU.mult), o_v)

            for l in range(DEPTH):
                norm(2 * l)
                turned(norm_no(l, 0))
                ada(ada_after(l, ("idxq", l, 0)))
                ada(ada_after(l, ("v", l, 0)))
                for h in range(IH):
                    ve.wait_ge(is_a, IH * l + h + 1)
                    if h:
                        own(is_v)
                    before = sc[:, 0, :] if h else ct[:, C_CAUSAL:C_CAUSAL + SQ]
                    r = relu[:, h % 2, :]
                    stt(sc[:, 0, 0:P], r[:, 0:P], iw[:, 0, h:h + 1], before[:, 0:P], ALU.mult, ALU.add)
                    signal(stt(sc[:, 0, P:SQ], r[:, P:SQ], iw[:, 1, h:h + 1], before[:, P:SQ], ALU.mult, ALU.add), is_v)
                own(is_v)
                ada(ada_after(l, ("v", l, 1)))
                for h in range(NH):
                    ve.wait_ge(z_p, NH * l + h + 1)
                    signal(tt(zb[:, h, :], bank[4 + h][:, 0:SQ], ct[:, C_STICK:C_STICK + SQ], ALU.add), z_v)
                own(z_v)
                ve.wait_ge(ze_a, 3 * l + 3)
                for h in range(NH):
                    signal(stt(eb[:, h, :], zb[:, h, :], 0.0, eb[:, h, :], ALU.max, ALU.add), sp_r)
                ada(ada_after(l, ("v", l, 2)))
                for t in range(DSA_K // 8):
                    a, b = sc[:, t % 2, :], sc[:, 1 - t % 2, :]
                    for lo, hi in ((0, P), (P, SQ)):
                        then(nc.vector.max(v8, a[:, lo:hi]))
                        then(nc.vector.match_replace(b[:, lo:hi], v8, a[:, lo:hi], TAKEN))
                then(ts(selm, sc[:, 0, :], TAKEN / 2, BIG, ALU.is_gt, ALU.mult))
                own(sp_r)
                for h in range(NH):
                    ve.wait_ge(suf_p, NH * l + h + 1)
                    signal(tt(zb[:, h, :], zb[:, h, :], bank[4 + h][:, 0:SQ], ALU.add), stT_v)
                ve.wait_ge(o_p, 13 * l + 1)
                signal(nc.vector.tensor_copy(xn[:, :, 0:T], bank[3][:, :].rearrange("p (b n) -> p b n", b=2)), o_v)
                heads(l, 0, NH)
                heads(l, NH, ALIBI)
                own(o_v)
                o2 = hT.rearrange("p c n -> p (c n)")
                of = xn.rearrange("p b n -> p (b n)")
                then(tt(o2, of, of, ALU.mult))
                signal(nc.vector.tensor_reduce(st[:, 8:40], o2.rearrange("p (a d) -> p a d", d=HD), AX_X, ALU.add), hr_v)
                ve.wait_ge(hq_a, l + 1)
                then(nc.vector.reciprocal(st[:, 8:40], st[:, 8:40]))
                o3 = of.rearrange("p (a d) -> p a d", d=HD)
                signal(tt(o3, o3, st[:, 8:40].unsqueeze(2).to_broadcast([P, 32, HD]), ALU.mult), on_v)
                turned(norm_no(l, 1))
                for n in range(4):
                    ve.wait_ge(wo_p, 4 * l + n + 1)
                    add_to_x(0, n // 2, n % 2, n)
                own(x_v)
                norm(2 * l + 1)
                turned(norm_no(l, 2))
                if l == 0:
                    n = 0
                    for j in range(FJ):
                        if j >= 2:
                            ve.wait_ge(y_p, j - 1)
                        for t in range(ff_tiles(j)):
                            ve.wait_ge(sg_a, n + 1)
                            signal(tt(ffT[:, j % 2, t, :], fsg[:, n % 2, :], bank[n % 2][:, T:2 * T], ALU.mult), h_v)
                            n += 1
                        if j < 5:
                            ada([("ada", 1, 2 * j), ("ada", 1, 2 * j + 1)])
                    ve.wait_ge(y_p, FJ)
                    for n in range(4):
                        add_to_x(1, n // 2, n % 2, n)
                    own(x_v)

            ve.wait_ge(r_p, 1)
            then(nc.vector.tensor_copy(lg, bank[0][:, 0:2 * NE].rearrange("p (b e) -> p b e", b=2)))
            for b in range(2):
                then(nc.vector.max(top[:, b, :], lg[:, b, :]))
                then(nc.vector.max_index(topi[:, b, :], top[:, b, :], lg[:, b, :]))
            then(nc.vector.tensor_copy(topf, topi[:, :, :]))
            for b in range(2):
                for k in range(2):
                    then(ts(oh[:, b, k, :], ct[:, C_IOTA:C_IOTA + NE], topf[:, b, k:k + 1], None, ALU.is_equal))
            signal(tt(chosen, oh[:, :, 0, :], oh[:, :, 1, :], ALU.add), sel_v)
            signal(tt(gt[:, :, 0], top[:, :, 1], top[:, :, 0], ALU.subtract), r_v)
            ve.wait_ge(r_a, 1)
            then(ts(gt[:, :, 2], gt[:, :, 1], 1.0, None, ALU.add))
            then(nc.vector.reciprocal(gt[:, :, 2], gt[:, :, 2]))
            then(tt(gt[:, :, 3], gt[:, :, 1], gt[:, :, 2], ALU.mult))
            own(sel_v)
            for b in range(2):
                then(ts(gate[:, b, 0:NE], oh[:, b, 0, :], gt[:, b, 2:3], None, ALU.mult))
                then(stt(gate[:, b, 0:NE], oh[:, b, 1, :], gt[:, b, 3:4], gate[:, b, 0:NE], ALU.mult, ALU.add))
            ve.wait_ge(r_p, 2)
            then(tt(pos[:, :, 0:NE], bank[1][:, 0:2 * NE].rearrange("p (b e) -> p b e", b=2), chosen, ALU.mult))
            then(ts(over, bank[1][:, 2 * NE:3 * NE], float(P), None, ALU.is_gt))
            then(tt(key, over, ct[:, C_DESC:C_DESC + NE], ALU.mult))
            then(nc.vector.max(key8, key))
            for r in range(EXTRA):
                then(ts(roh[:, r, :], key, key8[:, r:r + 1], None, ALU.is_equal))
                for b in range(2):
                    for table, first in ((pos, -float(P)), (gate, 0.0)):
                        then(ttr(scr, table[:, b, 0:NE], roh[:, r, :], 1.0, first, ALU.mult, ALU.add,
                                 table[:, b, NE + r:NE + r + 1]))
            then(ts(nxf[:, 0:EXTRA], key8[:, 0:EXTRA], -1.0, float(NE), ALU.mult, ALU.add))
            then(ts(nxf[:, 0:EXTRA], nxf[:, 0:EXTRA], float(NE - 1), None, ALU.min))
            then(nc.vector.tensor_reduce(nxf[:, 3:4], over, AX_X, ALU.add))
            then(ts(nxf[:, 3:4], nxf[:, 3:4], float(NE), None, ALU.add))
            signal(nc.vector.memset(yacc, 0.0), yacc_v)
            signal(nc.vector.tensor_copy(route_i[:, :], nxf), route_v)
            own(route_v)
            rounds = ve.value_load(route_i[0:1, 3:4], min_val=NE, max_val=NR_MAX)
            with ve.Fori(0, rounds) as r:
                for b in range(2):
                    p_ = pos[:, b, bass.ds(r, 1)]
                    ts(sel01[:, b, :], ct[:, C_SLOT:C_SLOT + P], p_, None, ALU.is_equal)
                    last = ts(selg[:, b, :], ct[:, C_SLOT:C_SLOT + P], p_, gate[:, b, bass.ds(r, 1)],
                              ALU.is_equal, ALU.mult)
                last.then_inc(sel_v, 1)
                ve.wait_ge(gat_p, r + 1)
                for k in range(KC // 2):
                    ts(xsT[:, k, :], bank[4 + k // 4][:, (k % 4) * P:(k % 4 + 1) * P], acol[:, 1, 1, k:k + 1],
                       mcol[:, 1, 24 + k:25 + k], ALU.mult, ALU.add).then_inc(xsT_v, 1)
                ve.wait_ge(sgt_p, r + 1)
                nc.vector.tensor_copy(selgT, bank[6][:, 0:T]).then_inc(sgt_v, 1)
                for j in range(EJ):
                    ve.wait_ge(esg_a, EJ * r + j + 1)
                    if j >= 2:
                        ve.wait_ge(et_p, EJ * r + j - 1)
                    tt(hs[:, j % 2, :], sg[:, j % 2, :], bank[2 * (j % 2) + 1][:, :], ALU.mult).then_inc(eh_v, 1)
                ve.wait_ge(sct_p, r + 1)
                ve.wait_ge(yacc_v, 4 * r + 1)
                for b in range(2):
                    for hf in range(2):
                        y_ = yacc[:, b, hf * CW:(hf + 1) * CW]
                        tt(y_, y_, bank[2 * hf + b][:, :], ALU.add).then_inc(yacc_v, 1)
            ve.wait_ge(yacc_v, rounds * 4 + 1)
            for b in range(2):
                then(tt(yacc[:, b, :], yacc[:, b, :], gates[:, 1, :], ALU.mult))
                signal(tt(xs[:, b, :], xs[:, b, :], yacc[:, b, :], ALU.add), x_v)
            own(x_v)
            ve.wait_ge(sq_r, 5)
            then(nc.vector.reciprocal(st[:, 4:6], st[:, 2:4]))
            ve.wait_ge(s_gfin, 16)
            stt(xn[:, 0, :], xs[:, 0, :], st[:, 4:5], gfin, ALU.mult, ALU.mult)
            stt(xn[:, 1, :], xs[:, 1, :], st[:, 5:6], gfin, ALU.mult, ALU.mult).then_inc(fin_v, 1)

        @block.scalar
        def _(ae):
            act = nc.scalar.activation
            eps, one = epst[:, 0:1], epst[:, 1:2]

            def norm(no, x_ready):
                x_ready()
                act(xn[:, 0, :], xs[:, 0, :], ACT.Square, accum_out=st[:, 0:1])
                act(xn[:, 1, :], xs[:, 1, :], ACT.Square, accum_out=st[:, 1:2]).then_inc(ss_r, 1)
                ae.wait_ge(ss_r, no + 1)
                act(st[:, 2:4], st[:, 0:2], ACT.Sqrt, bias=eps, scale=1.0 / D).then_inc(sq_r, 1)

            def turned(no, scales):
                l, which = no // 3, no % 3
                ae.wait_ge(ada_c, scales)
                for k in (2, 3, 6, 7):
                    g = k // 2
                    ae.wait_ge(tr_p, 4 * no + g + 1)
                    src = bank[4 + g][:, (k % 2) * T:(k % 2 + 1) * T]
                    if which == 1:
                        ins = act(hT[:, k, :], src, ACT.Copy, scale=cols[:, 128 + 8 * l + k:129 + 8 * l + k])
                    else:
                        w = which // 2
                        ins = act(hT[:, k, :], src, ACT.Identity, scale=acol[:, l, w, k:k + 1],
                                  bias=mcol[:, l, 24 * w + k:24 * w + k + 1])
                    ins.then_inc(tr_a, 1)

            def copied(G, dst, src, scale=1.0):
                ae.wait_ge(proj_p, G + 1)
                act(dst, src, ACT.Copy, scale=scale).then_inc(proj_c, 1)

            def qk(l, m, tiles):
                for t in tiles:
                    G = 25 * l + 5 + 5 * m + t
                    copied(G, qkT[:, m % 2, t, :], bank[G % 2][:, 0:T], 1.0 if t >= 2 else (-0.125 if m else 0.125))

            def v(l, m):
                G = 25 * l + 9 + 5 * m
                dst = vAB[:, m] if m < 2 else vCD[:, m - 2]
                copied(G, dst, bank[G % 2][:, :].rearrange("p (b n) -> p b n", b=2))

            def exps(l, n0, n1):
                for n in range(n0, n1):
                    N = ALIBI * l + n
                    ae.wait_ge(n_v, N + 1)
                    if n >= 2:
                        ae.wait_ge(pt_p, N - 1)
                    act(ex[:, n % 2, 0:P], nb[:, n % 2, 0:P], ACT.Exp, bias=mn[:, 0, n:n + 1], scale=-1.0,
                        accum_out=den[:, 0, n:n + 1])
                    act(ex[:, n % 2, P:SQ], nb[:, n % 2, P:SQ], ACT.Exp, bias=mn[:, 1, n:n + 1], scale=-1.0,
                        accum_out=den[:, 1, n:n + 1]).then_inc(e_a, 1)

            ae.wait_ge(setup_c, 1)
            act(cond[:, :], cols[:, 144:152], ACT.Silu).then_inc(cond_r, 1)
            for l in range(DEPTH):
                norm(2 * l, (lambda: ae.wait_ge(x_v, 8)) if l else (lambda: ae.wait_ge(s_x, 16)))
                turned(norm_no(l, 0), 22 if l else 4)
                for t in range(4):
                    G = 25 * l + t
                    copied(G, iq[:, t, :], bank[G % 2][:, 0:T])
                G = 25 * l + 4
                ae.wait_ge(proj_p, G + 1)
                act(ik, bank[G % 2][:, 0:T], ACT.Copy)
                act(iw.rearrange("p b h -> p (b h)"), bank[G % 2][:, T:T + 2 * IH], ACT.Copy,
                    scale=float(HD ** -0.5 * IH ** -0.5)).then_inc(proj_c, 1)
                qk(l, 0, range(4))
                v(l, 0)
                for h in range(IH):
                    ae.wait_ge(is_p, IH * l + h + 1)
                    if h >= 2:
                        ae.wait_ge(is_v, IH * l + h - 1)
                    act(relu[:, h % 2, :], bank[4 + h % 4][:, 0:SQ], ACT.Relu).then_inc(is_a, 1)
                qk(l, 1, range(4))
                v(l, 1)
                qk(l, 2, range(3))
                ae.wait_ge(z_v, NH * (l + 1))
                act(eb[:, :, :], zb[:, :, :], ACT.Abs).then_inc(ze_a, 1)
                ae.wait_ge(ze_a, 3 * l + 1)
                act(eb[:, :, :], eb[:, :, :], ACT.Exp, scale=-1.0).then_inc(ze_a, 1)
                ae.wait_ge(ze_a, 3 * l + 2)
                act(eb[:, :, :], eb[:, :, :], ACT.Ln, bias=one).then_inc(ze_a, 1)
                qk(l, 2, range(3, 4))
                v(l, 2)
                for h in range(NH):
                    ae.wait_ge(stT_v, NH * l + h + 1)
                    act(zb[:, h, :], zb[:, h, :], ACT.Exp).then_inc(stA_a, 1)
                exps(l, 0, NH)
                qk(l, 3, range(4))
                v(l, 3)
                exps(l, NH, ALIBI)
                ae.wait_ge(hr_v, l + 1)
                act(st[:, 8:40], st[:, 8:40], ACT.Sqrt, bias=eps, scale=1.0 / HD).then_inc(hq_a, 1)
                turned(norm_no(l, 1), 24 if l else 12)
                norm(2 * l + 1, lambda: ae.wait_ge(x_v, 8 * l + 4))
                if l:
                    ae.dma_start(wr, w_router[0].rearrange("(c p) e -> p c e", p=P)).then_inc(s_wr, 16)
                turned(norm_no(l, 2), 24 if l else 12)
                if l == 0:
                    for n in range(FF // P):
                        ae.wait_ge(gu_p, n + 1)
                        if n >= 2:
                            ae.wait_ge(h_v, n - 1)
                        act(fsg[:, n % 2, :], bank[n % 2][:, 0:T], ACT.Silu).then_inc(sg_a, 1)
            ae.wait_ge(r_v, 1)
            act(gt[:, :, 1], gt[:, :, 0], ACT.Exp).then_inc(r_a, 1)
            ae.wait_ge(route_v, 1)
            rounds = ae.value_load(route_i[0:1, 3:4], min_val=NE, max_val=NR_MAX)
            with ae.Fori(0, rounds) as r:
                ae.wait_ge(gat_p, r + 1)
                for k in range(KC // 2, KC):
                    act(xsT[:, k, :], bank[4 + k // 4][:, (k % 4) * P:(k % 4 + 1) * P], ACT.Identity,
                        scale=acol[:, 1, 1, k:k + 1], bias=mcol[:, 1, 24 + k:25 + k]).then_inc(xsT_a, 1)
                for j in range(EJ + 1):
                    if j < EJ:
                        ae.wait_ge(egu_p, EJ * r + j + 1)
                        if j >= 2:
                            ae.wait_ge(eh_v, EJ * r + j - 1)
                        act(sg[:, j % 2, :], bank[2 * (j % 2)][:, :], ACT.Silu).then_inc(esg_a, 1)
                    if j:
                        ae.wait_ge(et_p, EJ * r + j)
                        if j >= 3:
                            ae.wait_ge(ey_p, EJ * r + j - 2)
                        act(hsT[:, (j - 1) % 2, :, :], bank[4 + (j - 1) % 2][:, :].rearrange("p (t n) -> p t n", t=4),
                            ACT.Copy).then_inc(et_a, 1)
                ae.wait_ge(ey_p, EJ * r + EJ)
                act(ys[:, 0:CW], bank[6][:, :], ACT.Copy)
                act(ys[:, CW:D], bank[7][:, :], ACT.Copy).then_inc(ys_a, 1)
            norm(4, lambda: ae.wait_ge(x_v, 14))


def kernel(**inputs):
    import concourse.bacc as bacc
    from concourse.bass_utils import run_bass_kernel_spmd

    names = ["x", "c", "w_ada", "b_ada", "g_mix", "w_in", "g_heads", "w_out", "g_ffn", "w_ff_gate", "w_ff_up",
             "w_ff_down", "w_router", "w_exp_gate", "w_exp_up", "w_exp_down", "g_final"]
    nc = bacc.Bacc("TRN2", target_bir_lowering=False, num_devices=1)
    arrays = {f"in_{n}": np.ascontiguousarray(inputs[n]) for n in names}
    arrays["ctab"], arrays["btab"] = constants()
    args = [nc.dram_tensor(n, a.shape, F32, kind="ExternalInput").ap() for n, a in arrays.items()]
    args.append(nc.dram_tensor("out", (1, T, D), F32, kind="ExternalOutput").ap())
    build(nc, *args)
    r = run_bass_kernel_spmd(nc, [arrays], core_ids=[0])
    return r.results[0]["out"]
```

```python
from contextlib import ExitStack

import numpy as np

import concourse.bass as bass
from concourse import mybir

F32 = mybir.dt.float32
I32 = mybir.dt.int32
U32 = mybir.dt.uint32
ALU = mybir.AluOpType
ACT = mybir.ActivationFunctionType
AX_X = mybir.AxisListType.X

P = 128
T = 256
D = 1024
KC = D // P
DEPTH = 2
HD = 64
NH = 4
MIX = 4
QKV = 3 * NH * HD
IH = 8
DSA_K = T // 4
FF = 2816
NE = 8
FE = 3584
BT = 64
NB = T // BT
EPS = 1e-6
CW = 512
HC = CW // 2
SLOTS = 7
FJ = -(-FF // CW)
EJ = FE // CW
BIG = 1e30
ARENA = 8800
TAKEN = -3e38
SQ = P + T
ALIBI = 12

C_IDENT, C_TRIU, C_NEGTRI, C_NEGONES, C_ONES, C_SLOT = (i * P for i in range(6))
C_STICK = C_SLOT + T
C_CAUSAL = C_STICK + SQ
C_IOTA = C_CAUSAL + SQ
C_END = C_IOTA + NE

ADA = 6 * D // CW
GATES = (4, 5, 10, 11)


def stream():
    out = [("ada", 0, i) for i in range(4)]
    for l in range(DEPTH):
        late = {("idxq", 0, 0): 4, ("qk", 0, 0): 5, ("qk", 0, 1): 6, ("qk", 0, 2): 7, ("qk", 0, 3): 8, ("v", 0, 3): 9,
                ("idxq", 1, 0): 9, ("qk", 1, 0): 10, ("qk", 1, 1): 11}
        keys = [("idxq", l, 0), ("idxkw", l, 0)] + [(kind, l, m) for m in range(MIX) for kind in ("qk", "v")]
        for key in keys:
            out.append(key)
            if key in late:
                out.append(("ada", l, late[key]))
        out += [("wout", l, 0), ("wout", l, 1)]
        if l == 0:
            rest = [("ada", 0, 10), ("ada", 0, 11)] + [("ada", 1, i) for i in range(9)]
            for j in range(FJ + 1):
                if j < FJ:
                    out += [("ffg", 0, j), ("ffu", 0, j)] + rest[2 * j:2 * j + 2]
                if j:
                    out.append(("ffd", 0, j - 1))
    return out


STREAM = stream()
ROUND = [x for j in range(EJ + 1) for x in
         ([("g", j), ("u", j)] if j < EJ else []) + ([("d", j - 1)] if j >= 1 else [])]
PLACE = {key: (i % SLOTS, i // SLOTS) for i, key in enumerate(STREAM)}
BASE = len(STREAM)
PER = len(ROUND) // SLOTS
assert len(ROUND) % SLOTS == 0
RPLACE = {key: ((BASE + i) % SLOTS, (BASE + i) // SLOTS) for i, key in enumerate(ROUND)}


def ada_after(l, at):
    i = STREAM.index(at) + 1
    out = []
    while i < len(STREAM) and STREAM[i][0] == "ada":
        out.append(STREAM[i])
        i += 1
    return out


ADA_ORDER = [k for k in STREAM if k[0] == "ada"]
ADA_NO = {k: n for n, k in enumerate(ADA_ORDER)}


UNITS = {1: [("half", 0)], 2: [("wide", 0)], 3: [("wide", 0), ("half", 2)], 4: [("wide", 0), ("wide", 2)]}


def items(nb):
    return [(u, c2) for u in UNITS[nb] for c2 in ((0, 1) if u[0] == "wide" else (None,))]


def scatter_no(unit):
    return unit[1] // 2 + (2 if unit[0] == "wide" else 0)


def constants():
    p = np.arange(P)[:, None]
    j = np.arange(P)[None, :]
    ct = np.zeros((P, C_END), np.float32)
    ct[:, C_IDENT:C_IDENT + P] = p == j
    ct[:, C_TRIU:C_TRIU + P] = p <= j
    ct[:, C_NEGTRI:C_NEGTRI + P] = -(p >= j).astype(np.float32)
    ct[:, C_NEGONES:C_NEGONES + P] = -1
    ct[:, C_ONES:C_ONES + P] = 1
    ct[:, C_SLOT:C_SLOT + T] = np.arange(1, T + 1)
    q = np.arange(T)[None, :]
    ct[:, C_STICK:C_STICK + T] = np.where(p < q, 0, -BIG)
    ct[:, C_STICK + T:C_STICK + SQ] = np.where(p < j, 0, -BIG)
    dist = np.concatenate([p - j, p + P - q], axis=1)
    ct[:, C_CAUSAL:C_CAUSAL + SQ] = np.where(dist >= 0, 0, -BIG)
    ct[:, C_IOTA:C_IOTA + NE] = np.arange(NE)
    windows = sum(((dist >= 0) & (dist % s == 0) & (dist <= w)).astype(np.float64)
                  for w, s in ((128, 1), (512, 4), (2048, 16)))
    bt = np.zeros((P, ALIBI, SQ), np.float32)
    for mixer in range(3):
        for h in range(NH):
            slope = 2.0 ** (-8.0 * (h * 3 + mixer + 1) / ALIBI)
            seen = windows if mixer == 1 else (dist >= 0).astype(np.float64)
            bt[:, mixer * NH + h] = np.where(seen > 0, slope * dist - np.log(np.maximum(seen, 1)), BIG)
    return ct, bt


def build(nc, x, c, w_ada, b_ada, g_mix, w_in, g_heads, w_out, g_ffn, w_ff_gate, w_ff_up, w_ff_down,
          w_router, w_exp_gate, w_exp_up, w_exp_down, g_final, ctab_in, btab_in, out):
    with ExitStack() as ctx:
        def sb(name, shape, dt=F32):
            return ctx.enter_context(nc.sbuf_tensor(name, shape, dt))

        def sem(name):
            return ctx.enter_context(nc.semaphore(name))

        ring = sb("ring", [P, SLOTS, KC * CW])
        ct = sb("ct", [P, C_END])
        bt = sb("bt", [P, ALIBI, SQ])
        xs = sb("xs", [P, 2, D])
        xn = sb("xn", [P, 2, D])
        hT = sb("hT", [P, KC, T])
        gates = sb("gates", [P, 2, D])
        acc = sb("acc", [P, CW])
        rows = sb("rows", [P, P])
        rows2 = sb("rows2", [24, P])
        cols = sb("cols", [P, 152])
        cond = sb("cond", [P, KC])
        mcol = sb("mcol", [P, DEPTH, 48])
        acol = sb("acol", [P, DEPTH, 2, KC])
        st = sb("st", [P, 64])
        epst = sb("epst", [P, 2])
        arena = sb("arena", [P, ARENA])

        class At:
            at = 0

        def part(n):
            At.at += n
            assert At.at <= ARENA
            return arena[:, At.at - n:At.at]

        qkT = part(2 * 4 * T).rearrange("p (b t n) -> p b t n", b=2, t=4)
        iq = part(4 * T).rearrange("p (t n) -> p t n", t=4)
        vAB = part(2 * 2 * T).rearrange("p (m b n) -> p m b n", m=2, b=2)
        vCD = iq.rearrange("p (m b) n -> p m b n", m=2)
        ik = part(T)
        sc = part(2 * SQ).rearrange("p (b n) -> p b n", b=2)
        selm = part(SQ)
        zb = part(NH * SQ).rearrange("p (h n) -> p h n", h=NH)
        eb = part(NH * SQ).rearrange("p (h n) -> p h n", h=NH)
        relu = zb[:, 0:2]
        neg = eb[:, 0:2]
        ex = eb[:, 2:4]
        pt = zb[:, 0:2]
        iw = part(16).rearrange("p (b h) -> p b h", b=2)
        v8 = part(8)
        mn = part(24).rearrange("p (b h) -> p b h", b=2)
        den = part(24).rearrange("p (b h) -> p b h", b=2)
        rden = part(24).rearrange("p (b h) -> p b h", b=2)
        At.at = 0
        ffT = part(2 * 4 * T).rearrange("p (b t n) -> p b t n", b=2, t=4)
        fsg = part(2 * T).rearrange("p (b n) -> p b n", b=2)
        At.at = 0
        xsT = part(KC * T).rearrange("p (c n) -> p c n", c=KC)
        ys = xsT.rearrange("p (b q) n -> p b (q n)", b=NB)
        sg = part(2 * HC).rearrange("p (b n) -> p b n", b=2)
        hs = part(2 * HC).rearrange("p (b n) -> p b n", b=2)
        hsT = part(2 * HC).rearrange("p (b t n) -> p b t n", b=2, t=2)
        yacc = part(2 * D).rearrange("p (b n) -> p b n", b=2)
        sel01 = part(2 * T).rearrange("p (b n) -> p b n", b=2)
        selg = part(2 * NB * P).rearrange("p (b q n) -> p b q n", b=2, q=NB)
        selgT = part(2 * T).rearrange("p (q n) -> p q n", q=2)
        lg = part(2 * NE).rearrange("p (b e) -> p b e", b=2)
        top = part(2 * NE).rearrange("p (b e) -> p b e", b=2)
        topi = sb("topi", [P, 2, 8], U32)
        topf = part(2 * NE).rearrange("p (b e) -> p b e", b=2)
        oh = part(4 * NE).rearrange("p (b k e) -> p b k e", b=2, k=2)
        chosen = part(2 * NE).rearrange("p (b e) -> p b e", b=2)
        gt = part(8).rearrange("p (b e) -> p b e", b=2)
        pos = part(2 * (NE + 1)).rearrange("p (b r) -> p b r", b=2)
        gate = part(2 * (NE + 1)).rearrange("p (b r) -> p b r", b=2)
        nblk = part(NE)
        wr = part(KC * NE).rearrange("p (c e) -> p c e", c=KC)
        route_i = sb("route_i", [P, NE], I32)
        gfin = bt[:, 0:3, :].rearrange("p a n -> p (a n)")[:, 0:D]

        bank = [ctx.enter_context(nc.psum_tensor(f"bank{i}", [P, CW], F32)) for i in range(8)]

        full = [sem(f"full{i}") for i in range(SLOTS)]
        s_const, s_tab, s_x, s_rows = sem("const_in"), sem("tables_in"), sem("x_in"), sem("rows_in")
        s_wr, s_gfin, s_out = sem("router_in"), sem("gfinal_in"), sem("out_done")
        setup_t, setup_c = sem("setup_transposed"), sem("setup_copied")
        cond_r = sem("cond_ready")
        acc_r, ada_p, ada_c = sem("ada_sums"), sem("ada_product"), sem("ada_copied")
        ss_r, sq_r, xn_r = sem("square_sums"), sem("root"), sem("xn_ready")
        tr_p, tr_v, tr_a = sem("transposed"), sem("transposed_copied_v"), sem("transposed_copied_a")
        proj_p, proj_c = sem("projected"), sem("projected_copied")
        is_p, is_a, is_v = sem("index_scores"), sem("index_relu"), sem("index_sum")
        z_p, z_v, sp_r = sem("stick_scores"), sem("stick_scores_copied"), sem("stick_softplus")
        ze_a = sem("stick_exp_ln")
        suf_p, stT_v, stA_a = sem("stick_suffix"), sem("stick_log_weights"), sem("stick_weights")
        s_p, n_v, e_a = sem("scores"), sem("biased_scores"), sem("exponentials")
        pt_p, pt_c = sem("weights_transposed"), sem("weights_copied")
        o_p, o_v = sem("mixer_output"), sem("mixer_output_copied")
        hr_v, hq_a, on_v = sem("head_square_sums"), sem("head_roots"), sem("heads_normed")
        wo_p, x_v = sem("mixed"), sem("x_updated")
        gu_p, sg_a, h_v, y_p = sem("gate_up"), sem("silu"), sem("hidden"), sem("ffn_out")
        r_p, r_v, r_a, route_v = sem("router_product"), sem("router_step"), sem("router_exp"), sem("routed")
        sel_v, gat_p, xsT_v, xsT_a = sem("one_hots"), sem("gathered"), sem("gathered_v"), sem("gathered_a")
        sgt_p, sgt_v = sem("scatter_transposed"), sem("scatter_matrix")
        egu_p, esg_a, eh_v = sem("expert_gate_up"), sem("expert_silu"), sem("expert_hidden")
        et_p, et_a, ey_p = sem("expert_hidden_t"), sem("expert_hidden_t_copied"), sem("expert_out")
        ys_a, sct_p, yacc_v = sem("expert_out_copied"), sem("scattered"), sem("y_summed")
        dv, fin_a, fin_v = sem("vector_chain"), sem("final_act"), sem("final_ready")

        ident = ct[:, C_IDENT:C_IDENT + P]
        ones = ct[:, C_ONES:C_ONES + P]

        def slot(key, n, place=PLACE):
            return ring[:, place[key][0], 0:KC * n].rearrange("p (c n) -> p c n", c=KC)

        def slot_rows(key, nr, place=PLACE):
            return ring[:, place[key][0], 0:nr * D].rearrange("p (c n) -> p c n", c=nr)

        def arrived(eng, key):
            s, u = PLACE[key]
            eng.wait_ge(full[s], 16 * (u + 1))

        def released(key):
            kind, l, i = key
            return {"ada": (acc_r, ADA_NO.get(key, 0) + 1), "idxq": (proj_p, 25 * l + 4), "idxkw": (proj_p, 25 * l + 5),
                    "qk": (proj_p, 25 * l + 9 + 5 * i), "v": (proj_p, 25 * l + 10 + 5 * i),
                    "wout": (wo_p, 4 * l + 2 * i + 2), "ffg": (gu_p, min(4 * i + 4, FF // P)),
                    "ffu": (gu_p, min(4 * i + 4, FF // P)), "ffd": (y_p, i + 1)}[kind]

        def value(nb, j, b):
            return NB * j + (b + 1 if b < nb - 1 else NB)

        def steps(nb, b):
            return 1 if b < nb - 1 else NB - nb + 1

        def norm_no(l, which):
            return 3 * l + which

        def ff_tiles(j):
            return (min(FF, (j + 1) * CW) - j * CW) // P

        block = ctx.enter_context(nc.Block())

        @block.sync
        def _(sp):
            def source(key):
                kind, l, i = key
                kview = lambda w, a, b: w[:, a:b].rearrange("(c p) n -> p c n", p=P)
                if kind == "ada":
                    return kview(w_ada[l], i * CW, (i + 1) * CW), slot(key, CW)
                if kind == "idxq":
                    return kview(w_in[l], MIX * QKV, MIX * QKV + CW), slot(key, CW)
                if kind == "idxkw":
                    a = MIX * QKV + CW
                    return kview(w_in[l], a, a + HD + IH), slot(key, HD + IH)
                if kind == "qk":
                    return kview(w_in[l], i * QKV, i * QKV + CW), slot(key, CW)
                if kind == "v":
                    return kview(w_in[l], i * QKV + CW, (i + 1) * QKV), slot(key, T)
                if kind == "wout":
                    return kview(w_out[l], i * CW, (i + 1) * CW), slot(key, CW)
                n = ff_tiles(i)
                if kind == "ffd":
                    return (w_ff_down[0, i * CW:i * CW + n * P, :].rearrange("(c p) n -> p c n", p=P),
                            slot_rows(key, n))
                return kview((w_ff_gate if kind == "ffg" else w_ff_up)[0], i * CW, i * CW + n * P), slot(key, n * P)

            def load(key):
                s, u = PLACE[key]
                n = STREAM.index(key)
                if n >= SLOTS:
                    sp.wait_ge(*released(STREAM[n - SLOTS]))
                src, dst = source(key)
                sp.dma_start(dst, src).then_inc(full[s], 16)

            sp.dma_start(rows[0:96, :], b_ada.rearrange("l (j p) -> (l j) p", p=P)).then_inc(s_rows, 16)
            sp.dma_start(rows[96:112, :], g_mix.rearrange("l (j p) -> (l j) p", p=P)).then_inc(s_rows, 16)
            sp.dma_start(rows[112:128, :], g_ffn.rearrange("l (j p) -> (l j) p", p=P)).then_inc(s_rows, 16)
            sp.dma_start(rows2[0:16, :], g_heads.rearrange("l (j a) d -> (l j) (a d)", a=2)).then_inc(s_rows, 16)
            sp.dma_start(rows2[16:24, :], c.rearrange("a (j p) -> (a j) p", p=P)).then_inc(s_rows, 16)
            sp.dma_start(ct[:, :], ctab_in).then_inc(s_const, 16)
            sp.dma_start(xs[:, :, :], x[0].rearrange("(b p) n -> p b n", p=P)).then_inc(s_x, 16)
            for n, key in enumerate(STREAM):
                load(key)
                if n == 5:
                    sp.dma_start(bt[:, :, :], btab_in).then_inc(s_tab, 16)

            def load_piece(r, expert, i, before):
                what, j = ROUND[i]
                s, u = RPLACE[what, j]
                if before:
                    sp.wait_ge(*released(STREAM[BASE + i - SLOTS]))
                else:
                    old, oj = ROUND[i - SLOTS]
                    last = r if i >= SLOTS else r - 1
                    sp.wait_ge(ey_p if old == "d" else egu_p, last * (NB * EJ) + NB * (oj + 1))
                if what == "d":
                    src = w_exp_down[0, bass.ds(expert, 1), j * CW:(j + 1) * CW, :]
                    dst = slot_rows((what, j), 4, RPLACE)
                else:
                    src = (w_exp_gate if what == "g" else w_exp_up)[0, bass.ds(expert, 1), :, j * CW:(j + 1) * CW]
                    dst = slot((what, j), CW, RPLACE)
                sp.dma_start(dst, src.rearrange("e (c p) n -> p (e c) n", p=P)).then_inc(full[s], 16)

            for i in range(SLOTS):
                load_piece(0, 0, i, True)
            with sp.Fori(0, NE - 1) as r:
                for i in range(SLOTS, len(ROUND)):
                    load_piece(r, r, i, False)
                for i in range(SLOTS):
                    load_piece(r + 1, r + 1, i, False)
            for i in range(SLOTS, len(ROUND)):
                load_piece(NE - 1, NE - 1, i, False)
            sp.wait_ge(n_v, DEPTH * ALIBI)
            sp.dma_start(gfin, g_final.rearrange("(a n) -> a n", a=1).to_broadcast([P, D])).then_inc(s_gfin, 16)
            sp.wait_ge(fin_v, 1)
            sp.dma_start(out[0].rearrange("(b p) n -> p b n", p=P), xn[:, :, :]).then_inc(s_out, 16)
            sp.wait_ge(s_out, 16)

        @block.tensor
        def _(pe):
            mm = nc.tensor.matmul

            def ada(key):
                n = ADA_NO[key]
                _, l, i = key
                pe.wait_ge(acc_r, n + 1)
                if n:
                    pe.wait_ge(ada_c, n)
                a = acc[:, :]
                if i in GATES:
                    mm(bank[2][:, :], ones, a, start=True, stop=True)
                    for t in range(4):
                        row = l * 48 + 4 * i + t
                        last = mm(bank[2][:, t * P:(t + 1) * P], ident[:, row:row + 1].to_broadcast([P, P]), rows[:, :],
                                  start=False, stop=True, skip_group_check=True)
                else:
                    for t in range(4):
                        last = mm(bank[2][:, t:t + 1], a[:, t * P:(t + 1) * P], ones[:, 0:1], start=True, stop=True)
                last.then_inc(ada_p, 1)

            def turn(no):
                if no % 3 == 1:
                    pe.wait_ge(on_v, no // 3 + 1)
                else:
                    pe.wait_ge(xn_r, 2 * (no // 3) + (no % 3 == 2) + 1)
                for g in range(4):
                    for cc in range(2):
                        for b in range(2):
                            ch = 2 * g + cc
                            last = nc.tensor.transpose(bank[4 + g][:, cc * T + b * P:cc * T + (b + 1) * P],
                                                       xn[:, b, ch * P:(ch + 1) * P], ident)
                    last.then_inc(tr_p, 1)

            def turned(no):
                pe.wait_ge(tr_v, 4 * (no + 1))
                pe.wait_ge(tr_a, 4 * (no + 1))

            def group(G):
                if G >= 2:
                    pe.wait_ge(proj_c, G - 1)
                return bank[G % 2]

            pe.wait_ge(s_const, 16)
            pe.wait_ge(s_rows, 80)
            nc.tensor.transpose(bank[4][:, 0:P], rows[:, :], ident)
            nc.tensor.transpose(bank[4][:, P:P + 24], rows2[:, :], ident[0:24, 0:24]).then_inc(setup_t, 1)
            for i in range(4):
                ada(("ada", 0, i))

            for l in range(DEPTH):
                def tiles(key, g0, n, w_cols):
                    arrived(pe, key)
                    w = slot(key, w_cols)
                    for t in range(n):
                        G = 25 * l + g0 + t
                        o = group(G)
                        for k in range(KC):
                            last = mm(o[:, 0:T], w[:, k, t * P:(t + 1) * P], hT[:, k, :],
                                      start=(k == 0), stop=(k == KC - 1))
                        last.then_inc(proj_p, 1)

                turn(norm_no(l, 0))
                turned(norm_no(l, 0))
                tiles(("idxq", l, 0), 0, 4, CW)
                for key in ada_after(l, ("idxq", l, 0)):
                    ada(key)
                arrived(pe, ("idxkw", l, 0))
                w = slot(("idxkw", l, 0), HD + IH)
                o = group(25 * l + 4)
                for half in (0, 64):
                    for k in range(KC):
                        mm(o[half:half + HD, 0:T], w[:, k, 0:HD], hT[:, k, :], start=(k == 0), stop=(k == KC - 1))
                for b in range(2):
                    for k in range(KC):
                        last = mm(o[:, T + b * IH:T + (b + 1) * IH], hT[:, k, b * P:(b + 1) * P], w[:, k, HD:HD + IH],
                                  start=(k == 0), stop=(k == KC - 1))
                last.then_inc(proj_p, 1)

                def project(m):
                    tiles(("qk", l, m), 5 + 5 * m, 4, CW)
                    for k in ada_after(l, ("qk", l, m)):
                        ada(k)
                    key = ("v", l, m)
                    arrived(pe, key)
                    w = slot(key, T)
                    o = group(25 * l + 9 + 5 * m)
                    for b in range(2):
                        for k in range(KC):
                            last = mm(o[:, b * T:(b + 1) * T], hT[:, k, b * P:(b + 1) * P], w[:, k, :],
                                      start=(k == 0), stop=(k == KC - 1))
                    last.then_inc(proj_p, 1)
                    for k in ada_after(l, key):
                        ada(k)

                def half(h):
                    return slice(HD * (h % 2), HD * (h % 2) + HD)

                def values(m):
                    return vAB[:, m] if m < 2 else vCD[:, m - 2]

                project(0)
                pe.wait_ge(proj_c, 25 * l + 5)
                for h in range(IH):
                    if h >= 4:
                        pe.wait_ge(is_a, IH * l + h - 3)
                    o = bank[4 + h % 4]
                    mm(o[:, 0:P], iq[half(h), h // 2, 0:P], ik[half(h), 0:P], start=True, stop=True)
                    mm(o[:, P:SQ], iq[half(h), h // 2, P:T], ik[half(h), :], start=True, stop=True).then_inc(is_p, 1)
                project(1)
                for h in range(NH):
                    pe.wait_ge(is_a, IH * l + 5 + h)
                    pe.wait_ge(proj_c, 25 * l + 9)
                    q, k = qkT[half(h), 0, h // 2, :], qkT[half(h), 0, 2 + h // 2, :]
                    mm(bank[4 + h][:, 0:T], k[:, 0:P], q, start=True, stop=True)
                    mm(bank[4 + h][:, T:SQ], k[:, P:T], q[:, P:T], start=True, stop=True).then_inc(z_p, 1)
                project(2)
                for h in range(NH):
                    pe.wait_ge(sp_r, NH * l + h + 1)
                    o = bank[4 + h]
                    mm(o[:, 0:T], ct[:, C_NEGTRI:C_NEGTRI + P], eb[:, h, 0:T], start=True, stop=True)
                    mm(o[:, P:T], ct[:, C_NEGONES:C_NEGONES + P], eb[:, h, T:SQ], start=False, stop=True,
                       skip_group_check=True)
                    mm(o[:, T:SQ], ct[:, C_NEGTRI:C_NEGTRI + P], eb[:, h, T:SQ], start=True, stop=True).then_inc(suf_p, 1)

                def pv(m, h, wt, o):
                    v = values(m)
                    mm(o[:, h * HD:(h + 1) * HD], wt[:, 0:P], v[:, 0, h * HD:(h + 1) * HD], start=True, stop=True)
                    dst = o[:, T + h * HD:T + (h + 1) * HD]
                    mm(dst, wt[:, P:T], v[:, 0, h * HD:(h + 1) * HD], start=True, stop=False)
                    return mm(dst, wt[:, T:SQ], v[:, 1, h * HD:(h + 1) * HD], start=False, stop=True)

                def out_bank(m):
                    if 4 * l + m:
                        pe.wait_ge(o_v, 4 * l + m)

                for h in range(NH):
                    pe.wait_ge(stA_a, NH * l + h + 1)
                    if h == 0:
                        out_bank(0)
                    last = pv(0, h, zb[:, h, :], bank[3])
                last.then_inc(o_p, 1)

                def score(n):
                    m, h = 1 + n // NH, n % NH
                    N = ALIBI * l + n
                    pe.wait_ge(proj_c, 25 * l + 9 + 5 * m)
                    if n >= 2:
                        pe.wait_ge(n_v, N - 1)
                    else:
                        pe.wait_ge(stT_v, NH * (l + 1))
                    o = bank[4 + n % 2]
                    q, k = qkT[half(h), m % 2, h // 2, :], qkT[half(h), m % 2, 2 + h // 2, :]
                    mm(o[:, 0:P], q[:, 0:P], k[:, 0:P], start=True, stop=True)
                    mm(o[:, P:SQ], q[:, P:T], k, start=True, stop=True).then_inc(s_p, 1)

                def turn_weights(n):
                    N = ALIBI * l + n
                    pe.wait_ge(e_a, N + 1)
                    if n >= 2:
                        pe.wait_ge(pt_c, N - 1)
                    for t in range(3):
                        last = nc.tensor.transpose(bank[6 + n % 2][:, t * P:(t + 1) * P],
                                                   ex[:, n % 2, t * P:(t + 1) * P], ident)
                    last.then_inc(pt_p, 1)

                def apply(n):
                    m, h = 1 + n // NH, n % NH
                    pe.wait_ge(pt_c, ALIBI * l + n + 1)
                    if h == 0:
                        out_bank(m)
                    pv(m, h, pt[:, n % 2, :], bank[3]).then_inc(o_p, 1)

                def softmax_heads(n0, n1):
                    for n in range(n0, n1 + 2):
                        if n < n1:
                            score(n)
                        if n0 <= n - 1 < n1:
                            turn_weights(n - 1)
                        if n - 2 >= n0:
                            apply(n - 2)

                softmax_heads(0, NH)
                project(3)
                softmax_heads(NH, ALIBI)
                turn(norm_no(l, 1))
                turned(norm_no(l, 1))
                for hf in range(2):
                    key = ("wout", l, hf)
                    arrived(pe, key)
                    w = slot(key, CW)
                    for b in range(2):
                        for k in range(KC):
                            last = mm(bank[4 + 2 * hf + b][:, :], hT[:, k, b * P:(b + 1) * P], w[:, k, :],
                                      start=(k == 0), stop=(k == KC - 1))
                        last.then_inc(wo_p, 1)
                turn(norm_no(l, 2))
                turned(norm_no(l, 2))
                if l == 0:
                    n = 0
                    for j in range(FJ + 1):
                        if j < FJ:
                            arrived(pe, ("ffg", 0, j))
                            arrived(pe, ("ffu", 0, j))
                            w = [slot((kind, 0, j), ff_tiles(j) * P) for kind in ("ffg", "ffu")]
                            for t in range(ff_tiles(j)):
                                if n >= 2:
                                    pe.wait_ge(h_v, n - 1)
                                for a in range(2):
                                    for k in range(KC):
                                        last = mm(bank[n % 2][:, a * T:(a + 1) * T], w[a][:, k, t * P:(t + 1) * P],
                                                  hT[:, k, :], start=(k == 0), stop=(k == KC - 1))
                                last.then_inc(gu_p, 1)
                                n += 1
                                if t % 2:
                                    ada(ada_after(l, ("ffu", 0, j))[t // 2])
                        if j:
                            key = ("ffd", 0, j - 1)
                            arrived(pe, key)
                            w = slot_rows(key, ff_tiles(j - 1))
                            pe.wait_ge(h_v, min(4 * j, FF // P))
                            for r in range(ff_tiles(j - 1)):
                                for b in range(2):
                                    for hf in range(2):
                                        last = mm(bank[4 + 2 * hf + b][:, :], ffT[:, (j - 1) % 2, r, b * P:(b + 1) * P],
                                                  w[:, r, hf * CW:(hf + 1) * CW], start=(j == 1 and r == 0),
                                                  stop=(j == FJ and r == ff_tiles(j - 1) - 1))
                            last.then_inc(y_p, 1)

            pe.wait_ge(s_wr, 16)
            for b in range(2):
                for k in range(KC):
                    last = mm(bank[0][:, b * NE:(b + 1) * NE], hT[:, k, b * P:(b + 1) * P], wr[:, k, :],
                              start=(k == 0), stop=(k == KC - 1))
            last.then_inc(r_p, 1)
            pe.wait_ge(sel_v, 1)
            mm(bank[1][:, 0:NE], ct[:, C_TRIU:C_TRIU + P], chosen[:, 0, :], start=True, stop=True)
            mm(bank[1][:, NE:2 * NE], ones, chosen[:, 0, :], start=True, stop=False)
            mm(bank[1][:, NE:2 * NE], ct[:, C_TRIU:C_TRIU + P], chosen[:, 1, :], start=False, stop=True)
            mm(bank[1][:, 2 * NE:3 * NE], ones, chosen[:, 0, :], start=True, stop=False)
            mm(bank[1][:, 2 * NE:3 * NE], ones, chosen[:, 1, :], start=False, stop=True).then_inc(r_p, 1)

            pe.wait_ge(route_v, 1)

            def expert(r, nb):
                base = r * (NB * EJ)
                for k in range(KC):
                    for b in range(2):
                        last = mm(bank[4 + k // 2][:, (k % 2) * T:(k % 2) * T + nb * BT], xn[:, b, k * P:(k + 1) * P],
                                  sel01[:, b, 0:nb * BT], start=(b == 0), stop=(b == 1))
                last.then_inc(gat_p, 1)
                pe.wait_ge(yacc_v, 4 * r + 1)
                for n, unit in enumerate(UNITS[nb]):
                    for b in range(2):
                        last = nc.tensor.transpose(bank[2 + n][:, b * P:(b + 1) * P],
                                                   selg[:, b, scatter_no(unit), :], ident)
                last.then_inc(sgt_p, 1)
                pe.wait_ge(xsT_v, 4 * r + 4)
                pe.wait_ge(xsT_a, 4 * r + 4)
                seq = [(j, q) for j in range(EJ) for q in range(nb)]
                for i in range(len(seq) + 2):
                    if i < len(seq):
                        j, q = seq[i]
                        if i >= 2:
                            pe.wait_ge(eh_v, base + value(nb, *seq[i - 2]))
                        for a, what in enumerate("gu"):
                            if q == 0:
                                s, u = RPLACE[what, j]
                                pe.wait_ge(full[s], r * (16 * PER) + 16 * (u + 1))
                            w = slot((what, j), CW, RPLACE)
                            (kind, q0), wide_half = items(nb)[q]
                            for k in range(KC):
                                if kind == "wide":
                                    last = mm(bank[i % 2][:, a * HC:(a + 1) * HC], xsT[:, k, q0 * BT:(q0 + 2) * BT],
                                              w[:, k, wide_half * HC:(wide_half + 1) * HC],
                                              start=(k == 0), stop=(k == KC - 1))
                                    continue
                                for c2 in range(2):
                                    last = mm(bank[i % 2][BT * c2:BT * (c2 + 1), a * HC:(a + 1) * HC],
                                              xsT[:, k, q0 * BT:(q0 + 1) * BT], w[:, k, c2 * HC:(c2 + 1) * HC],
                                              start=(k == 0), stop=(k == KC - 1))
                        last.then_inc(egu_p, steps(nb, q))
                    if 1 <= i <= len(seq):
                        j, q = seq[i - 1]
                        pe.wait_ge(eh_v, base + value(nb, j, q))
                        if i == 1:
                            pe.wait_ge(sgt_v, r + 1)
                        if i >= 3:
                            pe.wait_ge(et_a, base + value(nb, *seq[i - 3]))
                        for t in range(2):
                            last = nc.tensor.transpose(bank[2 + (i - 1) % 2][:, t * P:(t + 1) * P],
                                                       hs[:, (i - 1) % 2, t * P:(t + 1) * P], ident)
                        last.then_inc(et_p, steps(nb, q))
                    if i >= 2:
                        j, q = seq[i - 2]
                        pe.wait_ge(et_a, base + value(nb, j, q))
                        if q == 0:
                            s, u = RPLACE["d", j]
                            pe.wait_ge(full[s], r * (16 * PER) + 16 * (u + 1))
                        w = slot_rows(("d", j), 4, RPLACE)
                        (kind, q0), wide_half = items(nb)[q]
                        if kind == "wide":
                            for t in range(2):
                                n = 2 * wide_half + t
                                for hf in range(2):
                                    last = mm(bank[4 + q0 + hf][:, :], hsT[:, (i - 2) % 2, t, :],
                                              w[:, n, hf * CW:(hf + 1) * CW], start=(j == 0 and n == 0),
                                              stop=(j == EJ - 1 and n == 3))
                        else:
                            for n in range(4):
                                for c2 in range(2):
                                    last = mm(bank[4 + q0][BT * c2:BT * (c2 + 1), :],
                                              hsT[:, (i - 2) % 2, n % 2, (n // 2) * BT:(n // 2 + 1) * BT],
                                              w[:, n, c2 * CW:(c2 + 1) * CW], start=(j == 0 and n == 0),
                                              stop=(j == EJ - 1 and n == 3))
                        last.then_inc(ey_p, steps(nb, q))
                pe.wait_ge(ys_a, r + 1)
                for b in range(2):
                    for n, (kind, q0) in enumerate(UNITS[nb]):
                        for c2 in range(2):
                            part, y = ((slice(0, P), ys[:, q0 + c2, :]) if kind == "wide" else
                                       (slice(BT * c2, BT * (c2 + 1)), ys[BT * c2:BT * (c2 + 1), q0, :]))
                            last = mm(bank[2 * c2 + b][:, :], selgT[part, n, b * P:(b + 1) * P], y,
                                      start=(n == 0), stop=(n == len(UNITS[nb]) - 1))
                last.then_inc(sct_p, 1)

            with pe.Fori(0, NE) as r:
                blocks = pe.value_load(route_i[0:1, bass.ds(r, 1)], min_val=1, max_val=NB)
                pe.wait_ge(sel_v, r + 2)
                for nb in range(1, NB + 1):
                    with pe.If(blocks == nb):
                        expert(r, nb)

        @block.vector
        def _(ve):
            ts, tt, stt = nc.vector.tensor_scalar, nc.vector.tensor_tensor, nc.vector.scalar_tensor_tensor
            ttr = nc.vector.tensor_tensor_reduce
            count = {}

            def signal(ins, s):
                ins.then_inc(s, 1)
                count[s.name] = count.get(s.name, 0) + 1

            def own(s):
                ve.wait_ge(s, count[s.name])

            def then(ins):
                signal(ins, dv)
                own(dv)

            def ada_sum(key):
                n = ADA_NO[key]
                ve.wait_ge(cond_r, 1)
                if n:
                    ve.wait_ge(ada_p, n)
                arrived(ve, key)
                w = slot(key, CW)
                then(ts(acc[:, :], w[:, 0, :], cond[:, 0:1], None, ALU.mult))
                for k in range(1, KC):
                    ins = stt(acc[:, :], w[:, k, :], cond[:, k:k + 1], acc[:, :], ALU.mult, ALU.add)
                    if k < KC - 1:
                        then(ins)
                    else:
                        signal(ins, acc_r)

            def ada_take(key):
                _, l, i = key
                ve.wait_ge(ada_p, ADA_NO[key] + 1)
                if i in GATES:
                    if l:
                        own(x_v)
                    dst = gates[:, GATES.index(i) // 2, (i % 2) * CW:(i % 2 + 1) * CW]
                    signal(nc.vector.tensor_copy(dst, bank[2][:, :]), ada_c)
                    return
                part = mcol[:, l, 4 * i:4 * i + 4]
                ins = tt(part, bank[2][:, 0:4], cols[:, l * 48 + 4 * i:l * 48 + 4 * i + 4], ALU.add)
                if i // 2 in (1, 4):
                    then(ins)
                    w = i // 2 // 4
                    g0 = 96 + 16 * w + 8 * l + 4 * (i % 2)
                    ins = stt(acol[:, l, w, 4 * (i % 2):4 * (i % 2) + 4], part, 1.0, cols[:, g0:g0 + 4],
                              ALU.add, ALU.mult)
                signal(ins, ada_c)

            taken = [0]

            def ada_take_all(keys):
                while taken[0] <= ADA_NO[keys[-1]]:
                    ada_take(ADA_ORDER[taken[0]])
                    taken[0] += 1

            def ada(keys, wait=True):
                for key in keys:
                    if ADA_NO[key]:
                        ada_take_all([ADA_ORDER[ADA_NO[key] - 1]])
                    ada_sum(key)
                if wait and keys:
                    ada_take_all(keys)

            def norm(no):
                ve.wait_ge(sq_r, no + 1)
                then(nc.vector.reciprocal(st[:, 4:6], st[:, 2:4]))
                ts(xn[:, 0, :], xs[:, 0, :], st[:, 4:5], None, ALU.mult)
                signal(ts(xn[:, 1, :], xs[:, 1, :], st[:, 5:6], None, ALU.mult), xn_r)

            def turned(no):
                l, which = no // 3, no % 3
                if which != 1:
                    own(ada_c)
                for k in (0, 1, 4, 5):
                    g = k // 2
                    ve.wait_ge(tr_p, 4 * no + g + 1)
                    src = bank[4 + g][:, (k % 2) * T:(k % 2 + 1) * T]
                    if which == 1:
                        ins = ts(hT[:, k, :], src, cols[:, 128 + 8 * l + k:129 + 8 * l + k], None, ALU.mult)
                    else:
                        w = which // 2
                        ins = ts(hT[:, k, :], src, acol[:, l, w, k:k + 1],
                                 mcol[:, l, 24 * w + k:24 * w + k + 1], ALU.mult, ALU.add)
                    signal(ins, tr_v)

            def add_to_x(kind, hf, b, n):
                tmp = zb.rearrange("p h n -> p (h n)")[:, (n % 2) * CW:(n % 2 + 1) * CW]
                own(ada_c)
                if x_v.name in count:
                    own(x_v)
                then(tt(tmp, bank[4 + 2 * hf + b][:, :], gates[:, kind, hf * CW:(hf + 1) * CW], ALU.mult))
                part = xs[:, b, hf * CW:(hf + 1) * CW]
                signal(tt(part, part, tmp, ALU.add), x_v)

            nc.vector.memset(epst[:, 0:1], EPS)
            signal(nc.vector.memset(epst[:, 1:2], 1.0), dv)
            ve.wait_ge(setup_t, 1)
            signal(nc.vector.tensor_copy(cols[:, :], bank[4][:, 0:P + 24]), setup_c)
            own(setup_c)
            ada([("ada", 0, i) for i in range(4)])

            def heads(l, n0, n1):
                for n in range(n0, n1 + 2):
                    if n < n1:
                        N = ALIBI * l + n
                        ve.wait_ge(s_p, N + 1)
                        if n == 0 and l == 0:
                            ve.wait_ge(s_tab, 16)
                        if n >= 2:
                            ve.wait_ge(e_a, N - 1)
                        s = bank[4 + n % 2][:, 0:SQ]
                        dst = neg[:, n % 2, :]
                        if n < NH:
                            then(tt(dst, s, selm, ALU.add))
                            s = dst
                        ttr(dst[:, 0:P], s[:, 0:P], bt[:, n, 0:P], 1.0, 3e38, ALU.add, ALU.min, mn[:, 0, n:n + 1])
                        signal(ttr(dst[:, P:SQ], s[:, P:SQ], bt[:, n, P:SQ], 1.0, 3e38, ALU.add, ALU.min,
                                   mn[:, 1, n:n + 1]), n_v)
                    if n0 <= n - 1 < n1:
                        N = ALIBI * l + n - 1
                        ve.wait_ge(pt_p, N + 1)
                        if n - 1 >= 2:
                            ve.wait_ge(o_p, 13 * l + 1 + n - 2)
                        signal(nc.vector.tensor_copy(pt[:, (n - 1) % 2, :], bank[6 + (n - 1) % 2][:, 0:SQ]), pt_c)
                    if n - 2 >= n0 and (n - 2) % NH == NH - 1:
                        m = 1 + (n - 2) // NH
                        hh = slice(n - 2 - NH + 1, n - 1)
                        ve.wait_ge(o_p, 13 * l + 1 + n - 1)
                        then(nc.vector.reciprocal(rden[:, :, hh], den[:, :, hh]))
                        dst = xn[:, :, m * T:(m + 1) * T].rearrange("p b (h d) -> p b h d", h=NH)
                        src = bank[3][:, :].rearrange("p (b h d) -> p b h d", b=2, h=NH)
                        signal(tt(dst, src, rden[:, :, hh].unsqueeze(3).to_broadcast([P, 2, NH, HD]), ALU.mult), o_v)

            for l in range(DEPTH):
                norm(2 * l)
                turned(norm_no(l, 0))
                ada(ada_after(l, ("idxq", l, 0)), wait=False)
                ada(ada_after(l, ("qk", l, 0)), wait=False)
                for h in range(IH):
                    ve.wait_ge(is_a, IH * l + h + 1)
                    if h:
                        own(is_v)
                    before = sc[:, 0, :] if h else ct[:, C_CAUSAL:C_CAUSAL + SQ]
                    r = relu[:, h % 2, :]
                    stt(sc[:, 0, 0:P], r[:, 0:P], iw[:, 0, h:h + 1], before[:, 0:P], ALU.mult, ALU.add)
                    signal(stt(sc[:, 0, P:SQ], r[:, P:SQ], iw[:, 1, h:h + 1], before[:, P:SQ], ALU.mult, ALU.add), is_v)
                own(is_v)
                ada(ada_after(l, ("qk", l, 1)), wait=False)
                for h in range(NH):
                    ve.wait_ge(z_p, NH * l + h + 1)
                    signal(tt(zb[:, h, :], bank[4 + h][:, 0:SQ], ct[:, C_STICK:C_STICK + SQ], ALU.add), z_v)
                own(z_v)
                ve.wait_ge(ze_a, 3 * l + 3)
                for h in range(NH):
                    signal(stt(eb[:, h, :], zb[:, h, :], 0.0, eb[:, h, :], ALU.max, ALU.add), sp_r)
                ada(ada_after(l, ("qk", l, 2)), wait=False)
                for t in range(DSA_K // 8):
                    a, b = sc[:, t % 2, :], sc[:, 1 - t % 2, :]
                    for lo, hi in ((0, P), (P, SQ)):
                        then(nc.vector.max(v8, a[:, lo:hi]))
                        then(nc.vector.match_replace(b[:, lo:hi], v8, a[:, lo:hi], TAKEN))
                then(ts(selm, sc[:, 0, :], TAKEN / 2, BIG, ALU.is_gt, ALU.mult))
                own(sp_r)
                for h in range(NH):
                    ve.wait_ge(suf_p, NH * l + h + 1)
                    signal(tt(zb[:, h, :], zb[:, h, :], bank[4 + h][:, 0:SQ], ALU.add), stT_v)
                ve.wait_ge(o_p, 13 * l + 1)
                signal(nc.vector.tensor_copy(xn[:, :, 0:T], bank[3][:, :].rearrange("p (b n) -> p b n", b=2)), o_v)
                heads(l, 0, NH)
                ada(ada_after(l, ("qk", l, 3)), wait=False)
                ada(ada_after(l, ("v", l, 3)), wait=False)
                heads(l, NH, ALIBI)
                ada_take_all([("ada", 1, 11) if l else ("ada", 0, 9)])
                own(o_v)
                o2 = hT.rearrange("p c n -> p (c n)")
                of = xn.rearrange("p b n -> p (b n)")
                then(tt(o2, of, of, ALU.mult))
                signal(nc.vector.tensor_reduce(st[:, 8:40], o2.rearrange("p (a d) -> p a d", d=HD), AX_X, ALU.add), hr_v)
                ve.wait_ge(hq_a, l + 1)
                then(nc.vector.reciprocal(st[:, 8:40], st[:, 8:40]))
                o3 = of.rearrange("p (a d) -> p a d", d=HD)
                signal(tt(o3, o3, st[:, 8:40].unsqueeze(2).to_broadcast([P, 32, HD]), ALU.mult), on_v)
                turned(norm_no(l, 1))
                for n in range(4):
                    ve.wait_ge(wo_p, 4 * l + n + 1)
                    add_to_x(0, n // 2, n % 2, n)
                own(x_v)
                norm(2 * l + 1)
                turned(norm_no(l, 2))
                if l == 0:
                    n = 0
                    for j in range(FJ):
                        if j >= 2:
                            ve.wait_ge(y_p, j - 1)
                        for t in range(ff_tiles(j)):
                            ve.wait_ge(sg_a, n + 1)
                            signal(tt(ffT[:, j % 2, t, :], fsg[:, n % 2, :], bank[n % 2][:, T:2 * T], ALU.mult), h_v)
                            n += 1
                            if t % 2 == 0:
                                ada(ada_after(l, ("ffu", 0, j))[t // 2:t // 2 + 1], wait=False)
                    ada_take_all([("ada", 1, 8)])
                    ve.wait_ge(y_p, FJ)
                    for n in range(4):
                        add_to_x(1, n // 2, n % 2, n)
                    own(x_v)

            ve.wait_ge(r_p, 1)
            then(nc.vector.tensor_copy(lg, bank[0][:, 0:2 * NE].rearrange("p (b e) -> p b e", b=2)))
            for b in range(2):
                then(nc.vector.max(top[:, b, :], lg[:, b, :]))
                then(nc.vector.max_index(topi[:, b, :], top[:, b, :], lg[:, b, :]))
            then(nc.vector.tensor_copy(topf, topi[:, :, :]))
            for b in range(2):
                for k in range(2):
                    then(ts(oh[:, b, k, :], ct[:, C_IOTA:C_IOTA + NE], topf[:, b, k:k + 1], None, ALU.is_equal))
            signal(tt(chosen, oh[:, :, 0, :], oh[:, :, 1, :], ALU.add), sel_v)
            signal(tt(gt[:, :, 0], top[:, :, 1], top[:, :, 0], ALU.subtract), r_v)
            ve.wait_ge(r_a, 1)
            then(ts(gt[:, :, 2], gt[:, :, 1], 1.0, None, ALU.add))
            then(nc.vector.reciprocal(gt[:, :, 2], gt[:, :, 2]))
            then(tt(gt[:, :, 3], gt[:, :, 1], gt[:, :, 2], ALU.mult))
            own(sel_v)
            for b in range(2):
                then(ts(gate[:, b, 0:NE], oh[:, b, 0, :], gt[:, b, 2:3], None, ALU.mult))
                then(stt(gate[:, b, 0:NE], oh[:, b, 1, :], gt[:, b, 3:4], gate[:, b, 0:NE], ALU.mult, ALU.add))
            ve.wait_ge(r_p, 2)
            then(tt(pos[:, :, 0:NE], bank[1][:, 0:2 * NE].rearrange("p (b e) -> p b e", b=2), chosen, ALU.mult))
            then(ts(nblk, bank[1][:, 2 * NE:3 * NE], float(BT), 1.0, ALU.is_gt, ALU.add))
            for q in range(2, NB):
                then(stt(nblk, bank[1][:, 2 * NE:3 * NE], float(q * BT), nblk, ALU.is_gt, ALU.add))
            signal(nc.vector.memset(pos[:, :, NE:NE + 1], 0.0), dv)
            signal(nc.vector.memset(gate[:, :, NE:NE + 1], 0.0), dv)
            signal(nc.vector.memset(yacc, 0.0), yacc_v)
            own(dv)
            signal(nc.vector.tensor_copy(route_i[:, :], nblk), route_v)
            own(route_v)

            def one_hots(r):
                slots = ct[:, C_SLOT:C_SLOT + T]
                for b in range(2):
                    p_, g_ = pos[:, b, bass.ds(r, 1)], gate[:, b, bass.ds(r, 1)]
                    ts(sel01[:, b, :], slots, p_, None, ALU.is_equal)
                    for c2 in range(2):
                        ts(selg[:, b, 0:2, c2 * BT:(c2 + 1) * BT], slots.rearrange("p (q n) -> p q n", q=2)[:, :, 0:BT],
                           p_, g_, ALU.is_equal, ALU.mult)
                    last = ts(selg[:, b, 2:4, :].rearrange("p q n -> p (q n)"), slots, p_, g_, ALU.is_equal, ALU.mult)
                last.then_inc(sel_v, 1)

            def expert(r, nb):
                base = r * (NB * EJ)
                ve.wait_ge(gat_p, r + 1)
                for k in range(KC // 2):
                    ts(xsT[:, k, 0:nb * BT], bank[4 + k // 2][:, (k % 2) * T:(k % 2) * T + nb * BT],
                       acol[:, 1, 1, k:k + 1], mcol[:, 1, 24 + k:25 + k], ALU.mult, ALU.add).then_inc(xsT_v, 1)
                ve.wait_ge(sgt_p, r + 1)
                for n in range(len(UNITS[nb])):
                    last = nc.vector.tensor_copy(selgT[:, n, :], bank[2 + n][:, 0:T])
                last.then_inc(sgt_v, 1)
                seq = [(j, q) for j in range(EJ) for q in range(nb)]
                for i, (j, q) in enumerate(seq):
                    ve.wait_ge(esg_a, base + value(nb, j, q))
                    if i >= 2:
                        ve.wait_ge(et_p, base + value(nb, *seq[i - 2]))
                    tt(hs[:, i % 2, :], sg[:, i % 2, :], bank[i % 2][:, HC:2 * HC], ALU.mult)\
                        .then_inc(eh_v, steps(nb, q))

            one_hots(0)
            with ve.Fori(0, NE) as r:
                blocks = ve.value_load(route_i[0:1, bass.ds(r, 1)], min_val=1, max_val=NB)
                for nb in range(1, NB + 1):
                    with ve.If(blocks == nb):
                        expert(r, nb)
                one_hots(r + 1)
                ve.wait_ge(sct_p, r + 1)
                ve.wait_ge(yacc_v, 4 * r + 1)
                for b in range(2):
                    for hf in range(2):
                        y_ = yacc[:, b, hf * CW:(hf + 1) * CW]
                        tt(y_, y_, bank[2 * hf + b][:, :], ALU.add).then_inc(yacc_v, 1)
            ve.wait_ge(yacc_v, 4 * NE + 1)
            for b in range(2):
                then(tt(yacc[:, b, :], yacc[:, b, :], gates[:, 1, :], ALU.mult))
                signal(tt(xs[:, b, :], xs[:, b, :], yacc[:, b, :], ALU.add), x_v)
            own(x_v)
            ve.wait_ge(sq_r, 5)
            then(nc.vector.reciprocal(st[:, 4:6], st[:, 2:4]))
            ve.wait_ge(s_gfin, 16)
            stt(xn[:, 0, :], xs[:, 0, :], st[:, 4:5], gfin, ALU.mult, ALU.mult)
            stt(xn[:, 1, :], xs[:, 1, :], st[:, 5:6], gfin, ALU.mult, ALU.mult).then_inc(fin_v, 1)

        @block.scalar
        def _(ae):
            act = nc.scalar.activation
            eps, one = epst[:, 0:1], epst[:, 1:2]

            def norm(no, x_ready):
                x_ready()
                act(xn[:, 0, :], xs[:, 0, :], ACT.Square, accum_out=st[:, 0:1])
                act(xn[:, 1, :], xs[:, 1, :], ACT.Square, accum_out=st[:, 1:2]).then_inc(ss_r, 1)
                ae.wait_ge(ss_r, no + 1)
                act(st[:, 2:4], st[:, 0:2], ACT.Sqrt, bias=eps, scale=1.0 / D).then_inc(sq_r, 1)

            def turned(no, scales):
                l, which = no // 3, no % 3
                ae.wait_ge(ada_c, ADA_NO[scales] + 1)
                for k in (2, 3, 6, 7):
                    g = k // 2
                    ae.wait_ge(tr_p, 4 * no + g + 1)
                    src = bank[4 + g][:, (k % 2) * T:(k % 2 + 1) * T]
                    if which == 1:
                        ins = act(hT[:, k, :], src, ACT.Copy, scale=cols[:, 128 + 8 * l + k:129 + 8 * l + k])
                    else:
                        w = which // 2
                        ins = act(hT[:, k, :], src, ACT.Identity, scale=acol[:, l, w, k:k + 1],
                                  bias=mcol[:, l, 24 * w + k:24 * w + k + 1])
                    ins.then_inc(tr_a, 1)

            def copied(G, dst, src, scale=1.0):
                ae.wait_ge(proj_p, G + 1)
                act(dst, src, ACT.Copy, scale=scale).then_inc(proj_c, 1)

            def qk(l, m, tiles):
                for t in tiles:
                    G = 25 * l + 5 + 5 * m + t
                    copied(G, qkT[:, m % 2, t, :], bank[G % 2][:, 0:T], 1.0 if t >= 2 else (-0.125 if m else 0.125))

            def v(l, m):
                G = 25 * l + 9 + 5 * m
                dst = vAB[:, m] if m < 2 else vCD[:, m - 2]
                copied(G, dst, bank[G % 2][:, :].rearrange("p (b n) -> p b n", b=2))

            def exps(l, n0, n1):
                for n in range(n0, n1):
                    N = ALIBI * l + n
                    ae.wait_ge(n_v, N + 1)
                    if n >= 2:
                        ae.wait_ge(pt_p, N - 1)
                    act(ex[:, n % 2, 0:P], neg[:, n % 2, 0:P], ACT.Exp, bias=mn[:, 0, n:n + 1], scale=-1.0,
                        accum_out=den[:, 0, n:n + 1])
                    act(ex[:, n % 2, P:SQ], neg[:, n % 2, P:SQ], ACT.Exp, bias=mn[:, 1, n:n + 1], scale=-1.0,
                        accum_out=den[:, 1, n:n + 1]).then_inc(e_a, 1)

            ae.wait_ge(setup_c, 1)
            act(cond[:, :], cols[:, 144:152], ACT.Silu).then_inc(cond_r, 1)
            for l in range(DEPTH):
                norm(2 * l, (lambda: ae.wait_ge(x_v, 8)) if l else (lambda: ae.wait_ge(s_x, 16)))
                turned(norm_no(l, 0), ("ada", l, 3))
                for t in range(4):
                    G = 25 * l + t
                    copied(G, iq[:, t, :], bank[G % 2][:, 0:T])
                G = 25 * l + 4
                ae.wait_ge(proj_p, G + 1)
                act(ik, bank[G % 2][:, 0:T], ACT.Copy)
                act(iw.rearrange("p b h -> p (b h)"), bank[G % 2][:, T:T + 2 * IH], ACT.Copy,
                    scale=float(HD ** -0.5 * IH ** -0.5)).then_inc(proj_c, 1)
                qk(l, 0, range(4))
                v(l, 0)
                for h in range(IH):
                    ae.wait_ge(is_p, IH * l + h + 1)
                    if h >= 2:
                        ae.wait_ge(is_v, IH * l + h - 1)
                    act(relu[:, h % 2, :], bank[4 + h % 4][:, 0:SQ], ACT.Relu).then_inc(is_a, 1)
                qk(l, 1, range(4))
                v(l, 1)
                qk(l, 2, range(3))
                ae.wait_ge(z_v, NH * (l + 1))
                act(eb[:, :, :], zb[:, :, :], ACT.Abs).then_inc(ze_a, 1)
                ae.wait_ge(ze_a, 3 * l + 1)
                act(eb[:, :, :], eb[:, :, :], ACT.Exp, scale=-1.0).then_inc(ze_a, 1)
                ae.wait_ge(ze_a, 3 * l + 2)
                act(eb[:, :, :], eb[:, :, :], ACT.Ln, bias=one).then_inc(ze_a, 1)
                qk(l, 2, range(3, 4))
                v(l, 2)
                for h in range(NH):
                    ae.wait_ge(stT_v, NH * l + h + 1)
                    act(zb[:, h, :], zb[:, h, :], ACT.Exp).then_inc(stA_a, 1)
                exps(l, 0, NH)
                qk(l, 3, range(4))
                v(l, 3)
                exps(l, NH, ALIBI)
                ae.wait_ge(hr_v, l + 1)
                act(st[:, 8:40], st[:, 8:40], ACT.Sqrt, bias=eps, scale=1.0 / HD).then_inc(hq_a, 1)
                turned(norm_no(l, 1), ("ada", l, 9))
                norm(2 * l + 1, lambda: ae.wait_ge(x_v, 8 * l + 4))
                if l:
                    ae.dma_start(wr, w_router[0].rearrange("(c p) e -> p c e", p=P)).then_inc(s_wr, 16)
                turned(norm_no(l, 2), ("ada", l, 9))
                if l == 0:
                    for n in range(FF // P):
                        ae.wait_ge(gu_p, n + 1)
                        if n >= 2:
                            ae.wait_ge(h_v, n - 1)
                        act(fsg[:, n % 2, :], bank[n % 2][:, 0:T], ACT.Silu).then_inc(sg_a, 1)
            ae.wait_ge(r_v, 1)
            act(gt[:, :, 1], gt[:, :, 0], ACT.Exp).then_inc(r_a, 1)
            ae.wait_ge(route_v, 1)

            def expert(r, nb):
                base = r * (NB * EJ)
                ae.wait_ge(gat_p, r + 1)
                for k in range(KC // 2, KC):
                    act(xsT[:, k, 0:nb * BT], bank[4 + k // 2][:, (k % 2) * T:(k % 2) * T + nb * BT], ACT.Identity,
                        scale=acol[:, 1, 1, k:k + 1], bias=mcol[:, 1, 24 + k:25 + k]).then_inc(xsT_a, 1)
                seq = [(j, q) for j in range(EJ) for q in range(nb)]
                for i in range(len(seq) + 1):
                    if i < len(seq):
                        ae.wait_ge(egu_p, base + value(nb, *seq[i]))
                        if i >= 2:
                            ae.wait_ge(eh_v, base + value(nb, *seq[i - 2]))
                        act(sg[:, i % 2, :], bank[i % 2][:, 0:HC], ACT.Silu).then_inc(esg_a, steps(nb, seq[i][1]))
                    if i:
                        ae.wait_ge(et_p, base + value(nb, *seq[i - 1]))
                        if i >= 3:
                            ae.wait_ge(ey_p, base + value(nb, *seq[i - 3]))
                        act(hsT[:, (i - 1) % 2, :, :],
                            bank[2 + (i - 1) % 2][:, 0:HC].rearrange("p (t n) -> p t n", t=2), ACT.Copy)\
                            .then_inc(et_a, steps(nb, seq[i - 1][1]))
                ae.wait_ge(ey_p, base + NB * EJ)
                for q in range(nb):
                    last = act(ys[:, q, :], bank[4 + q][:, :], ACT.Copy)
                last.then_inc(ys_a, 1)

            with ae.Fori(0, NE) as r:
                blocks = ae.value_load(route_i[0:1, bass.ds(r, 1)], min_val=1, max_val=NB)
                for nb in range(1, NB + 1):
                    with ae.If(blocks == nb):
                        expert(r, nb)
            norm(4, lambda: ae.wait_ge(x_v, 14))


def kernel(**inputs):
    import concourse.bacc as bacc
    from concourse.bass_utils import run_bass_kernel_spmd

    names = ["x", "c", "w_ada", "b_ada", "g_mix", "w_in", "g_heads", "w_out", "g_ffn", "w_ff_gate", "w_ff_up",
             "w_ff_down", "w_router", "w_exp_gate", "w_exp_up", "w_exp_down", "g_final"]
    nc = bacc.Bacc("TRN2", target_bir_lowering=False, num_devices=1)
    arrays = {f"in_{n}": np.ascontiguousarray(inputs[n]) for n in names}
    arrays["ctab"], arrays["btab"] = constants()
    args = [nc.dram_tensor(n, a.shape, F32, kind="ExternalInput").ap() for n, a in arrays.items()]
    args.append(nc.dram_tensor("out", (1, T, D), F32, kind="ExternalOutput").ap())
    build(nc, *args)
    r = run_bass_kernel_spmd(nc, [arrays], core_ids=[0])
    return r.results[0]["out"]
```

```python
from contextlib import ExitStack

import numpy as np

import concourse.bass as bass
from concourse import mybir

F32 = mybir.dt.float32
I32 = mybir.dt.int32
U32 = mybir.dt.uint32
ALU = mybir.AluOpType
ACT = mybir.ActivationFunctionType
AX_X = mybir.AxisListType.X

P = 128
T = 256
D = 1024
KC = D // P
DEPTH = 2
HD = 64
NH = 4
MIX = 4
QKV = 3 * NH * HD
IH = 8
DSA_K = T // 4
FF = 2816
NE = 8
FE = 3584
BT = 64
NB = T // BT
EPS = 1e-6
CW = 512
HC = CW // 2
SLOTS = 7
FJ = -(-FF // CW)
EJ = FE // CW
BIG = 1e30
ARENA = 8800
TAKEN = -3e38
SQ = P + T
ALIBI = 12

C_IDENT, C_ONES, C_TRIU, C_NEGTRI, C_NEGONES, C_SLOT = (i * P for i in range(6))
C_FIRST = 2 * P
C_STICK = C_SLOT + T
C_CAUSAL = C_STICK + SQ
C_IOTA = C_CAUSAL + SQ
C_END = C_IOTA + NE

ADA = 6 * D // CW
GATES = (4, 5, 10, 11)


STICK, SPARSE, DILATED, LOCAL = range(MIX)
SEQ = (STICK, DILATED, LOCAL, SPARSE)
SLOPE_NO = {SPARSE: 0, DILATED: 1, LOCAL: 2}
TOPK_STEPS = DSA_K // 8


def plan(l):
    late = iter(range(4, 10) if l == 0 else range(9, ADA))
    out = []

    def add(*steps):
        out.extend(steps)

    def proj(*g):
        add(*(("proj", x) for x in g))

    def ada_sum(whole=True):
        i = next(late, None)
        if i is not None:
            add(("sum", i))
            if whole:
                rest()

    def rest():
        add(*[("rest", i) for what, i in out if what == "sum" and ("rest", i) not in out])

    def ada():
        add(*[("ada", i) for what, i in out if what == "sum" and ("ada", i) not in out])

    def head(n, lo, hi):
        if lo <= n < hi:
            add(("score", n))
        if lo <= n - 2 < hi:
            add(("turn", n - 2))
        if lo <= n - 3 < hi:
            add(("pv", n - 3))
            if (n - 3) % NH == NH - 1:
                add(("out", 1 + (n - 3) // NH))

    ada_sum()
    proj(0, 1, 2, 3)
    ada()
    proj(4, 5)
    for t in range(4):
        add(("is", 2 * t), ("is", 2 * t + 1))
        if t < 3:
            proj(6 + t)
    ada_sum()
    proj(9, 10)
    ada()
    add(("z", 0), ("z", 1))
    proj(11)
    add(("z", 2), ("z", 3), ("ln", 0), *(("topk", t) for t in range(TOPK_STEPS // 2)))
    proj(12)
    add(("sp", 0))
    ada_sum()
    proj(13)
    add(*(("topk", t) for t in range(TOPK_STEPS // 2, TOPK_STEPS)))
    proj(14)
    ada()
    proj(15)
    add(*(("suf", h) for h in range(NH)))
    proj(16)
    add(("pva", 0))
    B1 = 2 * NH
    head(0, 0, B1)
    head(1, 0, B1)
    add(("out", 0))
    proj(17)
    ada_sum(False)
    head(2, 0, B1)
    rest()
    head(3, 0, B1)
    proj(18)
    ada()
    proj(19)
    head(4, 0, B1)
    head(5, 0, B1)
    ada_sum(False)
    proj(20)
    head(6, 0, B1)
    rest()
    head(7, 0, B1)
    proj(21)
    ada()
    head(8, 0, B1)
    proj(22)
    head(9, 0, B1)
    ada_sum()
    proj(23)
    head(10, 0, B1)
    proj(24)
    ada()
    for n in range(B1, ALIBI + 3):
        head(n, B1, ALIBI)
    return out


def group_key(l, g):
    if g < 5:
        return ("idxq" if g < 4 else "idxkw", l, 0)
    s, t = divmod(g - 5, 5)
    return ("qk" if t < 4 else "v", l, SEQ[s])


def stream():
    out = [("ada", 0, i) for i in range(4)]
    for l in range(DEPTH):
        for what, n in PLANS[l]:
            key = {"proj": lambda: group_key(l, n), "sum": lambda: ("ada", l, n)}.get(what, lambda: None)()
            if key and key not in out:
                out.append(key)
        out += [("wout", l, 0), ("wout", l, 1)]
        if l == 0:
            rest = [("ada", 0, 10), ("ada", 0, 11)] + [("ada", 1, i) for i in range(9)]
            for j in range(FJ + 1):
                if j < FJ:
                    out += [("ffg", 0, j), ("ffu", 0, j)] + rest[2 * j:2 * j + 2]
                if j:
                    out.append(("ffd", 0, j - 1))
    return out


PLANS = [plan(l) for l in range(DEPTH)]
STREAM = stream()
ROUND = [x for j in range(EJ + 1) for x in
         ([("g", j), ("u", j)] if j < EJ else []) + ([("d", j - 1)] if j >= 1 else [])]
PLACE = {key: (i % SLOTS, i // SLOTS) for i, key in enumerate(STREAM)}
BASE = len(STREAM)
ADA_SPLIT = 6
TURNS = (0, 1, 7, 2, 6, 3, 5, 4)
PER = len(ROUND) // SLOTS
assert len(ROUND) % SLOTS == 0
RPLACE = {key: ((BASE + i) % SLOTS, (BASE + i) // SLOTS) for i, key in enumerate(ROUND)}


def ada_after(l, at):
    i = STREAM.index(at) + 1
    out = []
    while i < len(STREAM) and STREAM[i][0] == "ada":
        out.append(STREAM[i])
        i += 1
    return out


ADA_ORDER = [k for k in STREAM if k[0] == "ada"]
ADA_NO = {k: n for n, k in enumerate(ADA_ORDER)}


UNITS = {1: [("half", 0)], 2: [("wide", 0)], 3: [("wide", 0), ("half", 2)], 4: [("wide", 0), ("wide", 2)]}


def items(nb):
    return [(u, c2) for u in UNITS[nb] for c2 in ((0, 1) if u[0] == "wide" else (None,))]


def scatter_no(unit):
    return unit[1] // 2 + (2 if unit[0] == "wide" else 0)


def constants():
    p = np.arange(P)[:, None]
    j = np.arange(P)[None, :]
    ct = np.zeros((P, C_END), np.float32)
    ct[:, C_IDENT:C_IDENT + P] = p == j
    ct[:, C_TRIU:C_TRIU + P] = p <= j
    ct[:, C_NEGTRI:C_NEGTRI + P] = -(p >= j).astype(np.float32)
    ct[:, C_NEGONES:C_NEGONES + P] = -1
    ct[:, C_ONES:C_ONES + P] = 1
    ct[:, C_SLOT:C_SLOT + T] = np.arange(1, T + 1)
    q = np.arange(T)[None, :]
    ct[:, C_STICK:C_STICK + T] = np.where(p < q, 0, -BIG)
    ct[:, C_STICK + T:C_STICK + SQ] = np.where(p < j, 0, -BIG)
    dist = np.concatenate([p - j, p + P - q], axis=1)
    ct[:, C_CAUSAL:C_CAUSAL + SQ] = np.where(dist >= 0, 0, -BIG)
    ct[:, C_IOTA:C_IOTA + NE] = np.arange(NE)
    windows = sum(((dist >= 0) & (dist % s == 0) & (dist <= w)).astype(np.float64)
                  for w, s in ((128, 1), (512, 4), (2048, 16)))
    bt = np.zeros((P, ALIBI, SQ), np.float32)
    for s, mixer in enumerate(SEQ[1:]):
        for h in range(NH):
            slope = 2.0 ** (-8.0 * (h * 3 + SLOPE_NO[mixer] + 1) / ALIBI)
            seen = windows if mixer == DILATED else (dist >= 0).astype(np.float64)
            bt[:, s * NH + h] = np.where(seen > 0, slope * dist - np.log(np.maximum(seen, 1)), BIG)
    return ct, bt


def build(nc, x, c, w_ada, b_ada, g_mix, w_in, g_heads, w_out, g_ffn, w_ff_gate, w_ff_up, w_ff_down,
          w_router, w_exp_gate, w_exp_up, w_exp_down, g_final, ctab_in, btab_in, out):
    with ExitStack() as ctx:
        def sb(name, shape, dt=F32):
            return ctx.enter_context(nc.sbuf_tensor(name, shape, dt))

        def sem(name):
            return ctx.enter_context(nc.semaphore(name))

        ring = sb("ring", [P, SLOTS, KC * CW])
        ct = sb("ct", [P, C_END])
        bt = sb("bt", [P, ALIBI, SQ])
        xs = sb("xs", [P, 2, D])
        xn = sb("xn", [P, 2, D])
        hT = sb("hT", [P, KC, T])
        gates = sb("gates", [P, 2, D])
        acc = sb("acc", [P, CW])
        rows = sb("rows", [P, P])
        rows2 = sb("rows2", [24, P])
        cols = sb("cols", [P, 152])
        cond = sb("cond", [P, KC])
        mcol = sb("mcol", [P, DEPTH, 48])
        acol = sb("acol", [P, DEPTH, 2, KC])
        st = sb("st", [P, 64])
        epst = sb("epst", [P, 2])
        arena = sb("arena", [P, ARENA])

        class At:
            at = 0

        def part(n):
            At.at += n
            assert At.at <= ARENA
            return arena[:, At.at - n:At.at]

        qkT = part(2 * 4 * T).rearrange("p (b t n) -> p b t n", b=2, t=4)
        iq = part(4 * T).rearrange("p (t n) -> p t n", t=4)
        vAB = part(2 * 2 * T).rearrange("p (m b n) -> p m b n", m=2, b=2)
        vCD = iq.rearrange("p (m b) n -> p m b n", m=2)
        ik = part(T)
        sc = part(2 * SQ).rearrange("p (b n) -> p b n", b=2)
        selm = part(SQ)
        zb = part(NH * SQ).rearrange("p (h n) -> p h n", h=NH)
        eb = part(NH * SQ).rearrange("p (h n) -> p h n", h=NH)
        relu = zb[:, 0:2]
        neg = eb[:, 0:2]
        ex = eb[:, 2:4]
        pt = zb[:, 0:2]
        sq = zb[:, 2:4].rearrange("p h n -> p (h n)")[:, 0:2 * T].rearrange("p (b n) -> p b n", b=2)
        iw = part(16).rearrange("p (b h) -> p b h", b=2)
        v8 = part(8)
        mn = part(24).rearrange("p (b h) -> p b h", b=2)
        den = part(24).rearrange("p (b h) -> p b h", b=2)
        rden = part(24).rearrange("p (b h) -> p b h", b=2)
        At.at = 0
        ffT = part(2 * 4 * T).rearrange("p (b t n) -> p b t n", b=2, t=4)
        fsg = part(2 * T).rearrange("p (b n) -> p b n", b=2)
        At.at = 0
        xsT = part(KC * T).rearrange("p (c n) -> p c n", c=KC)
        ys = xsT.rearrange("p (b q) n -> p b (q n)", b=NB)
        sg = part(2 * HC).rearrange("p (b n) -> p b n", b=2)
        hs = part(2 * HC).rearrange("p (b n) -> p b n", b=2)
        hsT = part(2 * HC).rearrange("p (b t n) -> p b t n", b=2, t=2)
        yacc = part(2 * D).rearrange("p (b n) -> p b n", b=2)
        sel01 = part(2 * T).rearrange("p (b n) -> p b n", b=2)
        selg = part(2 * NB * P).rearrange("p (b q n) -> p b q n", b=2, q=NB)
        selgT = part(2 * T).rearrange("p (q n) -> p q n", q=2)
        lg = part(2 * NE).rearrange("p (b e) -> p b e", b=2)
        top = part(2 * NE).rearrange("p (b e) -> p b e", b=2)
        topi = sb("topi", [P, 2, 8], U32)
        topf = part(2 * NE).rearrange("p (b e) -> p b e", b=2)
        oh = part(4 * NE).rearrange("p (b k e) -> p b k e", b=2, k=2)
        chosen = part(2 * NE).rearrange("p (b e) -> p b e", b=2)
        gt = part(8).rearrange("p (b e) -> p b e", b=2)
        pos = part(2 * (NE + 1)).rearrange("p (b r) -> p b r", b=2)
        gate = part(2 * (NE + 1)).rearrange("p (b r) -> p b r", b=2)
        nblk = part(NE)
        route = part(2 * (NE + 1)).rearrange("p (a r) -> p a r", a=2)
        rank = part(2 * NE).rearrange("p (a e) -> p a e", a=2)
        wr = part(KC * NE).rearrange("p (c e) -> p c e", c=KC)
        route_i = sb("route_i", [P, 2, NE + 1], I32)

        def expert_of(eng, r, last=NE - 1):
            return 0 if isinstance(r, int) and r == 0 else \
                eng.value_load(route_i[0:1, 0, bass.ds(r, 1)], min_val=0, max_val=last)

        def blocks_of(eng, r):
            return eng.value_load(route_i[0:1, 1, bass.ds(r, 1)], min_val=1, max_val=NB)

        gfin = bt[:, 0:3, :].rearrange("p a n -> p (a n)")[:, 0:D]

        bank = [ctx.enter_context(nc.psum_tensor(f"bank{i}", [P, CW], F32)) for i in range(8)]

        full = [sem(f"full{i}") for i in range(SLOTS)]
        s_const, s_const2 = sem("const_in"), sem("late_const_in")
        s_tab, s_x, s_rows = sem("tables_in"), sem("x_in"), sem("rows_in")
        s_wr, s_gfin, s_out = sem("router_in"), sem("gfinal_in"), sem("out_done")
        setup_t, setup_c = sem("setup_transposed"), sem("setup_copied")
        cond_r = sem("cond_ready")
        acc_r, ada_p, ada_c = sem("ada_sums"), sem("ada_product"), sem("ada_copied")
        ss_r, sq_r, xn_r = sem("square_sums"), sem("root"), sem("xn_ready")
        tr_p, tr_v, tr_a = sem("transposed"), sem("transposed_copied_v"), sem("transposed_copied_a")
        proj_p, proj_c = sem("projected"), sem("projected_copied")
        is_p, is_a, is_v = sem("index_scores"), sem("index_relu"), sem("index_sum")
        z_p, z_v, sp_r = sem("stick_scores"), sem("stick_scores_copied"), sem("stick_softplus")
        ze_a = sem("stick_exp_ln")
        suf_p, stT_v, stA_a = sem("stick_suffix"), sem("stick_log_weights"), sem("stick_weights")
        s_p, n_v, e_a = sem("scores"), sem("biased_scores"), sem("exponentials")
        pt_p, pt_c = sem("weights_transposed"), sem("weights_copied")
        o_p, o_v = sem("mixer_output"), sem("mixer_output_copied")
        hr_v, hq_a, on_v = sem("head_square_sums"), sem("head_roots"), sem("heads_normed")
        wo_p, x_v = sem("mixed"), sem("x_updated")
        gu_p, sg_a, h_v, y_p = sem("gate_up"), sem("silu"), sem("hidden"), sem("ffn_out")
        r_p, r_v, r_a, route_v = sem("router_product"), sem("router_step"), sem("router_exp"), sem("routed")
        sel_v, gat_p, xsT_v, xsT_a = sem("one_hots"), sem("gathered"), sem("gathered_v"), sem("gathered_a")
        sgt_p, sgt_v = sem("scatter_transposed"), sem("scatter_matrix")
        eg_p, egu_p, esg_a, eh_v = sem("expert_gate"), sem("expert_gate_up"), sem("expert_silu"), sem("expert_hidden")
        et_p, et_a, ey_p = sem("expert_hidden_t"), sem("expert_hidden_t_copied"), sem("expert_out")
        ys_a, sct_p, yacc_v = sem("expert_out_copied"), sem("scattered"), sem("y_summed")
        dv, fin_a, fin_v = sem("vector_chain"), sem("final_act"), sem("final_ready")

        ident = ct[:, C_IDENT:C_IDENT + P]
        ones = ct[:, C_ONES:C_ONES + P]

        def slot(key, n, place=PLACE):
            return ring[:, place[key][0], 0:KC * n].rearrange("p (c n) -> p c n", c=KC)

        def slot_rows(key, nr, place=PLACE):
            return ring[:, place[key][0], 0:nr * D].rearrange("p (c n) -> p c n", c=nr)

        def arrived(eng, key):
            s, u = PLACE[key]
            eng.wait_ge(full[s], 16 * (u + 1))

        def released(key):
            kind, l, i = key
            turn = SEQ.index(i) if kind in ("qk", "v") else 0
            return {"ada": (ada_p, ADA_NO.get(key, 0) + 1), "idxq": (proj_p, 25 * l + 4), "idxkw": (proj_p, 25 * l + 5),
                    "qk": (proj_p, 25 * l + 9 + 5 * turn), "v": (proj_p, 25 * l + 10 + 5 * turn),
                    "wout": (wo_p, 4 * l + 3 + i), "ffg": (gu_p, min(4 * i + 4, FF // P)),
                    "ffu": (gu_p, min(4 * i + 4, FF // P)), "ffd": (y_p, i + 1 + 3 * (i == FJ - 1))}[kind]

        def value(nb, j, b):
            return NB * j + (b + 1 if b < nb - 1 else NB)

        def steps(nb, b):
            return 1 if b < nb - 1 else NB - nb + 1

        def norm_no(l, which):
            return 3 * l + which

        def ff_tiles(j):
            return (min(FF, (j + 1) * CW) - j * CW) // P

        block = ctx.enter_context(nc.Block())

        @block.sync
        def _(sp):
            def source(key):
                kind, l, i = key
                kview = lambda w, a, b: w[:, a:b].rearrange("(c p) n -> p c n", p=P)
                if kind == "ada":
                    return kview(w_ada[l], i * CW, (i + 1) * CW), slot(key, CW)
                if kind == "idxq":
                    return kview(w_in[l], MIX * QKV, MIX * QKV + CW), slot(key, CW)
                if kind == "idxkw":
                    a = MIX * QKV + CW
                    return kview(w_in[l], a, a + HD + IH), slot(key, HD + IH)
                if kind == "qk":
                    return kview(w_in[l], i * QKV, i * QKV + CW), slot(key, CW)
                if kind == "v":
                    return kview(w_in[l], i * QKV + CW, (i + 1) * QKV), slot(key, T)
                if kind == "wout":
                    return kview(w_out[l], i * CW, (i + 1) * CW), slot(key, CW)
                n = ff_tiles(i)
                if kind == "ffd":
                    return (w_ff_down[0, i * CW:i * CW + n * P, :].rearrange("(c p) n -> p c n", p=P),
                            slot_rows(key, n))
                return kview((w_ff_gate if kind == "ffg" else w_ff_up)[0], i * CW, i * CW + n * P), slot(key, n * P)

            def load(key):
                s, u = PLACE[key]
                n = STREAM.index(key)
                if n >= SLOTS:
                    sp.wait_ge(*released(STREAM[n - SLOTS]))
                src, dst = source(key)
                sp.dma_start(dst, src).then_inc(full[s], 16)

            sp.dma_start(rows[0:96, :], b_ada.rearrange("l (j p) -> (l j) p", p=P)).then_inc(s_rows, 16)
            sp.dma_start(rows[96:112, :], g_mix.rearrange("l (j p) -> (l j) p", p=P)).then_inc(s_rows, 16)
            sp.dma_start(rows[112:128, :], g_ffn.rearrange("l (j p) -> (l j) p", p=P)).then_inc(s_rows, 16)
            sp.dma_start(rows2[0:16, :], g_heads.rearrange("l (j a) d -> (l j) (a d)", a=2)).then_inc(s_rows, 16)
            sp.dma_start(rows2[16:24, :], c.rearrange("a (j p) -> (a j) p", p=P)).then_inc(s_rows, 16)
            sp.dma_start(ct[:, 0:C_FIRST], ctab_in[:, 0:C_FIRST]).then_inc(s_const, 16)
            for n, key in enumerate(STREAM):
                load(key)
                if n == 1:
                    sp.dma_start(xs[:, :, :], x[0].rearrange("(b p) n -> p b n", p=P)).then_inc(s_x, 16)
                if n == 3:
                    sp.dma_start(ct[:, C_FIRST:C_END], ctab_in[:, C_FIRST:C_END]).then_inc(s_const2, 16)
                if n == 5:
                    sp.dma_start(bt[:, :, :], btab_in).then_inc(s_tab, 16)

            def load_piece(r, expert, i, before):
                what, j = ROUND[i]
                s, u = RPLACE[what, j]
                if before:
                    sp.wait_ge(*released(STREAM[BASE + i - SLOTS]))
                else:
                    old, oj = ROUND[i - SLOTS]
                    last = r if i >= SLOTS else r - 1
                    sp.wait_ge({"g": eg_p, "u": egu_p, "d": ey_p}[old], last * (NB * EJ) + NB * (oj + 1))
                if what == "d":
                    src = w_exp_down[0, bass.ds(expert, 1), j * CW:(j + 1) * CW, :]
                    dst = slot_rows((what, j), 4, RPLACE)
                else:
                    src = (w_exp_gate if what == "g" else w_exp_up)[0, bass.ds(expert, 1), :, j * CW:(j + 1) * CW]
                    dst = slot((what, j), CW, RPLACE)
                sp.dma_start(dst, src.rearrange("e (c p) n -> p (e c) n", p=P)).then_inc(full[s], 16)

            for i in range(SLOTS):
                load_piece(0, 0, i, True)
            sp.wait_ge(route_v, 2)
            with sp.Fori(0, NE - 1) as r:
                e = expert_of(sp, r)
                for i in range(SLOTS, len(ROUND)):
                    load_piece(r, e, i, False)
                e = expert_of(sp, r + 1)
                for i in range(SLOTS):
                    load_piece(r + 1, e, i, False)
            e = expert_of(sp, NE - 1)
            for i in range(SLOTS, len(ROUND)):
                load_piece(NE - 1, e, i, False)
            sp.wait_ge(n_v, DEPTH * ALIBI)
            sp.dma_start(gfin, g_final.rearrange("(a n) -> a n", a=1).to_broadcast([P, D])).then_inc(s_gfin, 16)
            for b in range(2):
                sp.wait_ge(fin_v, b + 1)
                sp.dma_start(out[0, b * P:(b + 1) * P, :], xn[:, b, :]).then_inc(s_out, 16)
            sp.wait_ge(s_out, 32)

        @block.tensor
        def _(pe):
            mm = nc.tensor.matmul

            def ada(key):
                n = ADA_NO[key]
                _, l, i = key
                if n:
                    pe.wait_ge(ada_c, n)
                if n < 4:
                    if n == 0:
                        pe.wait_ge(cond_r, 1)
                    arrived(pe, key)
                    for t in range(4):
                        for k in range(ADA_SPLIT, KC):
                            mm(bank[2][:, 4 + t:5 + t], slot(key, CW)[:, k, t * P:(t + 1) * P], cond[:, k:k + 1],
                               start=(k == ADA_SPLIT), stop=(k == KC - 1))
                pe.wait_ge(acc_r, n + 1)
                a = acc[:, :]
                if i in GATES:
                    mm(bank[2][:, :], ones, a, start=True, stop=True)
                    for t in range(4):
                        row = l * 48 + 4 * i + t
                        last = mm(bank[2][:, t * P:(t + 1) * P], ident[:, row:row + 1].to_broadcast([P, P]), rows[:, :],
                                  start=False, stop=True, skip_group_check=True)
                else:
                    for t in range(4):
                        last = mm(bank[2][:, t:t + 1], a[:, t * P:(t + 1) * P], ones[:, 0:1], start=True, stop=True)
                last.then_inc(ada_p, 1)

            def turn(no):
                if no % 3 != 1:
                    pe.wait_ge(xn_r, 4 * (no // 3) + 2 * (no % 3 == 2) + 2)
                for g in range(4):
                    if no % 3 == 1:
                        pe.wait_ge(on_v, MIX * (no // 3) + g + 1)
                    for cc in range(2):
                        for b in range(2):
                            ch = 2 * g + cc
                            last = nc.tensor.transpose(bank[4 + g][:, cc * T + b * P:cc * T + (b + 1) * P],
                                                       xn[:, b, ch * P:(ch + 1) * P], ident)
                    last.then_inc(tr_p, 1)

            def turned(no):
                pe.wait_ge(tr_v, 4 * (no + 1))
                pe.wait_ge(tr_a, 4 * (no + 1))

            def group(G):
                if G >= 2:
                    pe.wait_ge(proj_c, G - 1)
                return bank[G % 2]

            pe.wait_ge(s_const, 16)
            pe.wait_ge(s_rows, 80)
            nc.tensor.transpose(bank[4][:, 0:P], rows[:, :], ident)
            nc.tensor.transpose(bank[4][:, P:P + 24], rows2[:, :], ident[0:24, 0:24]).then_inc(setup_t, 1)
            for i in range(4):
                ada(("ada", 0, i))

            for l in range(DEPTH):
                turn(norm_no(l, 0))
                turned(norm_no(l, 0))

                def project(g):
                    key = group_key(l, g)
                    arrived(pe, key)
                    o = group(25 * l + g)
                    if key[0] == "idxkw":
                        w = slot(key, HD + IH)
                        for half in (0, 64):
                            for k in range(KC):
                                mm(o[half:half + HD, 0:T], w[:, k, 0:HD], hT[:, k, :], start=(k == 0), stop=(k == KC - 1))
                        for b in range(2):
                            for k in range(KC):
                                last = mm(o[:, T + b * IH:T + (b + 1) * IH], hT[:, k, b * P:(b + 1) * P],
                                          w[:, k, HD:HD + IH], start=(k == 0), stop=(k == KC - 1))
                    elif key[0] == "v":
                        w = slot(key, T)
                        for b in range(2):
                            for k in range(KC):
                                last = mm(o[:, b * T:(b + 1) * T], hT[:, k, b * P:(b + 1) * P], w[:, k, :],
                                          start=(k == 0), stop=(k == KC - 1))
                    else:
                        w = slot(key, CW)
                        t = g if key[0] == "idxq" else (g - 5) % 5
                        for k in range(KC):
                            last = mm(o[:, 0:T], w[:, k, t * P:(t + 1) * P], hT[:, k, :], start=(k == 0), stop=(k == KC - 1))
                    last.then_inc(proj_p, 1)

                def half(h):
                    return slice(HD * (h % 2), HD * (h % 2) + HD)

                def values(s):
                    return vAB[:, s] if s < 2 else vCD[:, s - 2]

                def index_scores(h):
                    if h == 0:
                        pe.wait_ge(proj_c, 25 * l + 5)
                    if h >= 4:
                        pe.wait_ge(is_a, IH * l + h - 3)
                    o = bank[4 + h % 4]
                    mm(o[:, 0:P], iq[half(h), h // 2, 0:P], ik[half(h), 0:P], start=True, stop=True)
                    mm(o[:, P:SQ], iq[half(h), h // 2, P:T], ik[half(h), :], start=True, stop=True).then_inc(is_p, 1)

                def stick_scores(h):
                    pe.wait_ge(is_a, IH * l + 5 + h)
                    pe.wait_ge(proj_c, 25 * l + 9)
                    q, k = qkT[half(h), 0, h // 2, :], qkT[half(h), 0, 2 + h // 2, :]
                    mm(bank[4 + h][:, 0:T], k[:, 0:P], q, start=True, stop=True)
                    mm(bank[4 + h][:, T:SQ], k[:, P:T], q[:, P:T], start=True, stop=True).then_inc(z_p, 1)

                def stick_sums(h):
                    if h == 0 and l == 0:
                        pe.wait_ge(s_const2, 16)
                    pe.wait_ge(sp_r, NH * l + h + 1)
                    o = bank[4 + h]
                    mm(o[:, 0:T], ct[:, C_NEGTRI:C_NEGTRI + P], eb[:, h, 0:T], start=True, stop=True)
                    mm(o[:, P:T], ct[:, C_NEGONES:C_NEGONES + P], eb[:, h, T:SQ], start=False, stop=True,
                       skip_group_check=True)
                    mm(o[:, T:SQ], ct[:, C_NEGTRI:C_NEGTRI + P], eb[:, h, T:SQ], start=True, stop=True).then_inc(suf_p, 1)

                def pv(m, h, wt, o):
                    v = values(m)
                    mm(o[:, h * HD:(h + 1) * HD], wt[:, 0:P], v[:, 0, h * HD:(h + 1) * HD], start=True, stop=True)
                    dst = o[:, T + h * HD:T + (h + 1) * HD]
                    mm(dst, wt[:, P:T], v[:, 0, h * HD:(h + 1) * HD], start=True, stop=False)
                    return mm(dst, wt[:, T:SQ], v[:, 1, h * HD:(h + 1) * HD], start=False, stop=True)

                def out_bank(m):
                    if 4 * l + m:
                        pe.wait_ge(o_v, 4 * l + m)

                def stick_out():
                    pe.wait_ge(proj_c, 25 * l + 10)
                    for h in range(NH):
                        pe.wait_ge(stA_a, NH * l + h + 1)
                        if h == 0:
                            out_bank(0)
                        last = pv(0, h, zb[:, h, :], bank[3])
                    last.then_inc(o_p, 1)

                def score(n):
                    m, h = 1 + n // NH, n % NH
                    N = ALIBI * l + n
                    pe.wait_ge(proj_c, 25 * l + 9 + 5 * m)
                    if n >= 2:
                        pe.wait_ge(n_v, N - 1)
                    else:
                        pe.wait_ge(stT_v, NH * (l + 1))
                    o = bank[4 + n % 2]
                    q, k = qkT[half(h), m % 2, h // 2, :], qkT[half(h), m % 2, 2 + h // 2, :]
                    mm(o[:, 0:P], q[:, 0:P], k[:, 0:P], start=True, stop=True)
                    mm(o[:, P:SQ], q[:, P:T], k, start=True, stop=True).then_inc(s_p, 1)

                def turn_weights(n):
                    N = ALIBI * l + n
                    pe.wait_ge(e_a, N + 1)
                    if n >= 2:
                        pe.wait_ge(pt_c, N - 1)
                    for t in range(3):
                        last = nc.tensor.transpose(bank[6 + n % 2][:, t * P:(t + 1) * P],
                                                   ex[:, n % 2, t * P:(t + 1) * P], ident)
                    last.then_inc(pt_p, 1)

                def apply(n):
                    m, h = 1 + n // NH, n % NH
                    pe.wait_ge(pt_c, ALIBI * l + n + 1)
                    if h == 0:
                        pe.wait_ge(proj_c, 25 * l + 10 + 5 * m)
                        out_bank(m)
                    pv(m, h, pt[:, n % 2, :], bank[3]).then_inc(o_p, 1)

                for what, n in PLANS[l]:
                    if what == "proj":
                        project(n)
                    elif what == "ada":
                        ada(("ada", l, n))
                    elif what == "is":
                        index_scores(n)
                    elif what == "z":
                        stick_scores(n)
                    elif what == "suf":
                        stick_sums(n)
                    elif what == "pva":
                        stick_out()
                    elif what == "score":
                        score(n)
                    elif what == "turn":
                        turn_weights(n)
                    elif what == "pv":
                        apply(n)
                turn(norm_no(l, 1))
                turned(norm_no(l, 1))
                for b in range(2):
                    for hf in range(2):
                        if b == 0:
                            arrived(pe, ("wout", l, hf))
                        w = slot(("wout", l, hf), CW)
                        for k in range(KC):
                            last = mm(bank[4 + 2 * hf + b][:, :], hT[:, k, b * P:(b + 1) * P], w[:, k, :],
                                      start=(k == 0), stop=(k == KC - 1))
                        last.then_inc(wo_p, 1)
                turn(norm_no(l, 2))
                turned(norm_no(l, 2))
                if l == 0:
                    n = 0
                    for j in range(FJ + 1):
                        if j < FJ:
                            arrived(pe, ("ffg", 0, j))
                            arrived(pe, ("ffu", 0, j))
                            w = [slot((kind, 0, j), ff_tiles(j) * P) for kind in ("ffg", "ffu")]
                            for t in range(ff_tiles(j)):
                                if n >= 2:
                                    pe.wait_ge(h_v, n - 1)
                                for a in range(2):
                                    for k in range(KC):
                                        last = mm(bank[n % 2][:, a * T:(a + 1) * T], w[a][:, k, t * P:(t + 1) * P],
                                                  hT[:, k, :], start=(k == 0), stop=(k == KC - 1))
                                last.then_inc(gu_p, 1)
                                n += 1
                                if t % 2:
                                    ada(ada_after(l, ("ffu", 0, j))[t // 2])
                        if j:
                            key = ("ffd", 0, j - 1)
                            arrived(pe, key)
                            w = slot_rows(key, ff_tiles(j - 1))
                            pe.wait_ge(h_v, min(4 * j, FF // P))
                            for b in range(2):
                                for hf in range(2):
                                    for r in range(ff_tiles(j - 1)):
                                        last = mm(bank[4 + 2 * hf + b][:, :], ffT[:, (j - 1) % 2, r, b * P:(b + 1) * P],
                                                  w[:, r, hf * CW:(hf + 1) * CW], start=(j == 1 and r == 0),
                                                  stop=(j == FJ and r == ff_tiles(j - 1) - 1))
                                    if j == FJ or (b, hf) == (1, 1):
                                        last.then_inc(y_p, 1)

            pe.wait_ge(s_wr, 16)
            for b in range(2):
                for k in range(KC):
                    last = mm(bank[0][:, b * NE:(b + 1) * NE], hT[:, k, b * P:(b + 1) * P], wr[:, k, :],
                              start=(k == 0), stop=(k == KC - 1))
            last.then_inc(r_p, 1)
            pe.wait_ge(sel_v, 1)
            mm(bank[1][:, 0:NE], ct[:, C_TRIU:C_TRIU + P], chosen[:, 0, :], start=True, stop=True)
            mm(bank[1][:, NE:2 * NE], ones, chosen[:, 0, :], start=True, stop=False)
            mm(bank[1][:, NE:2 * NE], ct[:, C_TRIU:C_TRIU + P], chosen[:, 1, :], start=False, stop=True)
            mm(bank[1][:, 2 * NE:3 * NE], ones, chosen[:, 0, :], start=True, stop=False)
            mm(bank[1][:, 2 * NE:3 * NE], ones, chosen[:, 1, :], start=False, stop=True).then_inc(r_p, 1)

            pe.wait_ge(route_v, 1)

            def expert(r, nb):
                base = r * (NB * EJ)
                for k in range(KC):
                    for b in range(2):
                        last = mm(bank[4 + k // 2][:, (k % 2) * T:(k % 2) * T + nb * BT], xn[:, b, k * P:(k + 1) * P],
                                  sel01[:, b, 0:nb * BT], start=(b == 0), stop=(b == 1))
                last.then_inc(gat_p, 1)
                pe.wait_ge(yacc_v, 4 * r + 1)
                for n, unit in enumerate(UNITS[nb]):
                    for b in range(2):
                        last = nc.tensor.transpose(bank[2 + n][:, b * P:(b + 1) * P],
                                                   selg[:, b, scatter_no(unit), :], ident)
                last.then_inc(sgt_p, 1)
                pe.wait_ge(xsT_v, 4 * r + 4)
                pe.wait_ge(xsT_a, 4 * r + 4)
                seq = [(j, q) for j in range(EJ) for q in range(nb)]

                def gate_up(i, a):
                    j, q = seq[i]
                    if a == 0 and i >= 2:
                        pe.wait_ge(eh_v, base + value(nb, *seq[i - 2]))
                    what = "gu"[a]
                    if q == 0:
                        s, u = RPLACE[what, j]
                        pe.wait_ge(full[s], r * (16 * PER) + 16 * (u + 1))
                    w = slot((what, j), CW, RPLACE)
                    (kind, q0), wide_half = items(nb)[q]
                    for k in range(KC):
                        if kind == "wide":
                            last = mm(bank[i % 2][:, a * HC:(a + 1) * HC], xsT[:, k, q0 * BT:(q0 + 2) * BT],
                                      w[:, k, wide_half * HC:(wide_half + 1) * HC], start=(k == 0), stop=(k == KC - 1))
                            continue
                        for c2 in range(2):
                            last = mm(bank[i % 2][BT * c2:BT * (c2 + 1), a * HC:(a + 1) * HC],
                                      xsT[:, k, q0 * BT:(q0 + 1) * BT], w[:, k, c2 * HC:(c2 + 1) * HC],
                                      start=(k == 0), stop=(k == KC - 1))
                    last.then_inc(egu_p if a else eg_p, steps(nb, q))

                def turn_hidden(i):
                    pe.wait_ge(eh_v, base + value(nb, *seq[i]))
                    if i == 0:
                        pe.wait_ge(sgt_v, r + 1)
                    if i >= 2:
                        pe.wait_ge(et_a, base + value(nb, *seq[i - 2]))
                    for t in range(2):
                        last = nc.tensor.transpose(bank[2 + i % 2][:, t * P:(t + 1) * P],
                                                   hs[:, i % 2, t * P:(t + 1) * P], ident)
                    last.then_inc(et_p, steps(nb, seq[i][1]))

                def down(i):
                    j, q = seq[i]
                    pe.wait_ge(et_a, base + value(nb, j, q))
                    if q == 0:
                        s, u = RPLACE["d", j]
                        pe.wait_ge(full[s], r * (16 * PER) + 16 * (u + 1))
                    w = slot_rows(("d", j), 4, RPLACE)
                    (kind, q0), wide_half = items(nb)[q]
                    if kind == "wide":
                        for t in range(2):
                            n = 2 * wide_half + t
                            for hf in range(2):
                                last = mm(bank[4 + q0 + hf][:, :], hsT[:, i % 2, t, :], w[:, n, hf * CW:(hf + 1) * CW],
                                          start=(j == 0 and n == 0), stop=(j == EJ - 1 and n == 3))
                    else:
                        for n in range(4):
                            for c2 in range(2):
                                last = mm(bank[4 + q0][BT * c2:BT * (c2 + 1), :],
                                          hsT[:, i % 2, n % 2, (n // 2) * BT:(n // 2 + 1) * BT],
                                          w[:, n, c2 * CW:(c2 + 1) * CW],
                                          start=(j == 0 and n == 0), stop=(j == EJ - 1 and n == 3))
                    last.then_inc(ey_p, steps(nb, q))

                for i in range(len(seq) + 1):
                    if i < len(seq):
                        gate_up(i, 0)
                    if i:
                        turn_hidden(i - 1)
                    if i < len(seq):
                        gate_up(i, 1)
                    if i:
                        down(i - 1)
                pe.wait_ge(ys_a, r + 1)
                for b in range(2):
                    for n, (kind, q0) in enumerate(UNITS[nb]):
                        for c2 in range(2):
                            part, y = ((slice(0, P), ys[:, q0 + c2, :]) if kind == "wide" else
                                       (slice(BT * c2, BT * (c2 + 1)), ys[BT * c2:BT * (c2 + 1), q0, :]))
                            last = mm(bank[2 * c2 + b][:, :], selgT[part, n, b * P:(b + 1) * P], y,
                                      start=(n == 0), stop=(n == len(UNITS[nb]) - 1))
                last.then_inc(sct_p, 1)

            with pe.Fori(0, NE) as r:
                blocks = blocks_of(pe, r)
                pe.wait_ge(sel_v, r + 2)
                for nb in range(1, NB + 1):
                    with pe.If(blocks == nb):
                        expert(r, nb)

        @block.vector
        def _(ve):
            ts, tt, stt = nc.vector.tensor_scalar, nc.vector.tensor_tensor, nc.vector.scalar_tensor_tensor
            ttr = nc.vector.tensor_tensor_reduce
            count = {}

            def signal(ins, s):
                ins.then_inc(s, 1)
                count[s.name] = count.get(s.name, 0) + 1

            def own(s):
                ve.wait_ge(s, count[s.name])

            def then(ins):
                signal(ins, dv)
                own(dv)

            def ada_sum(key, chunks=None):
                n = ADA_NO[key]
                end = ADA_SPLIT if n < 4 else KC
                w = slot(key, CW)
                for k in chunks or range(end):
                    if k:
                        ins = stt(acc[:, :], w[:, k, :], cond[:, k:k + 1], acc[:, :], ALU.mult, ALU.add)
                    else:
                        ve.wait_ge(cond_r, 1)
                        if n:
                            ve.wait_ge(ada_p, n)
                        arrived(ve, key)
                        ins = ts(acc[:, :], w[:, 0, :], cond[:, 0:1], None, ALU.mult)
                    if k < end - 1:
                        then(ins)
                    else:
                        signal(ins, acc_r)

            def ada_take(key):
                _, l, i = key
                ve.wait_ge(ada_p, ADA_NO[key] + 1)
                if i in GATES:
                    if l:
                        own(x_v)
                    dst = gates[:, GATES.index(i) // 2, (i % 2) * CW:(i % 2 + 1) * CW]
                    signal(nc.vector.tensor_copy(dst, bank[2][:, :]), ada_c)
                    return
                part = mcol[:, l, 4 * i:4 * i + 4]
                ins = tt(part, bank[2][:, 0:4], cols[:, l * 48 + 4 * i:l * 48 + 4 * i + 4], ALU.add)
                if ADA_NO[key] < 4:
                    then(ins)
                    ins = tt(part, part, bank[2][:, 4:8], ALU.add)
                if i // 2 in (1, 4):
                    then(ins)
                    w = i // 2 // 4
                    g0 = 96 + 16 * w + 8 * l + 4 * (i % 2)
                    ins = stt(acol[:, l, w, 4 * (i % 2):4 * (i % 2) + 4], part, 1.0, cols[:, g0:g0 + 4],
                              ALU.add, ALU.mult)
                signal(ins, ada_c)

            taken = [0]

            def ada_take_all(keys):
                while taken[0] <= ADA_NO[keys[-1]]:
                    ada_take(ADA_ORDER[taken[0]])
                    taken[0] += 1

            def ada(keys, wait=True):
                for key in keys:
                    if ADA_NO[key]:
                        ada_take_all([ADA_ORDER[ADA_NO[key] - 1]])
                    ada_sum(key)
                if wait and keys:
                    ada_take_all(keys)

            def norm(no, b):
                ve.wait_ge(sq_r, 2 * no + b + 1)
                then(nc.vector.reciprocal(st[:, 4 + b:5 + b], st[:, 2 + b:3 + b]))
                signal(ts(xn[:, b, :], xs[:, b, :], st[:, 4 + b:5 + b], None, ALU.mult), xn_r)

            def turned(no):
                l, which = no // 3, no % 3
                if which != 1:
                    own(ada_c)
                for k in (0, 1, 4, 5):
                    g = k // 2
                    ve.wait_ge(tr_p, 4 * no + g + 1)
                    src = bank[4 + g][:, (k % 2) * T:(k % 2 + 1) * T]
                    if which == 1:
                        ins = ts(hT[:, k, :], src, cols[:, 128 + 8 * l + k:129 + 8 * l + k], None, ALU.mult)
                    else:
                        w = which // 2
                        ins = ts(hT[:, k, :], src, acol[:, l, w, k:k + 1],
                                 mcol[:, l, 24 * w + k:24 * w + k + 1], ALU.mult, ALU.add)
                    signal(ins, tr_v)

            def add_to_x(kind, hf, b, n):
                tmp = zb.rearrange("p h n -> p (h n)")[:, (n % 2) * CW:(n % 2 + 1) * CW]
                own(ada_c)
                if count.get(x_v.name, 0) > 1:
                    ve.wait_ge(x_v, count[x_v.name] - 1)
                then(tt(tmp, bank[4 + 2 * hf + b][:, :], gates[:, kind, hf * CW:(hf + 1) * CW], ALU.mult))
                part = xs[:, b, hf * CW:(hf + 1) * CW]
                signal(tt(part, part, tmp, ALU.add), x_v)

            nc.vector.memset(epst[:, 0:1], EPS)
            signal(nc.vector.memset(epst[:, 1:2], 1.0), dv)
            ve.wait_ge(setup_t, 1)
            signal(nc.vector.tensor_copy(cols[:, :], bank[4][:, 0:P + 24]), setup_c)
            own(setup_c)
            ada([("ada", 0, i) for i in range(4)])

            def biased(l, n):
                N = ALIBI * l + n
                ve.wait_ge(s_p, N + 1)
                if N == 0:
                    ve.wait_ge(s_tab, 16)
                if n >= 2:
                    ve.wait_ge(e_a, N - 1)
                s = bank[4 + n % 2][:, 0:SQ]
                dst = neg[:, n % 2, :]
                if SEQ[1 + n // NH] == SPARSE:
                    then(tt(dst, s, selm, ALU.add))
                    s = dst
                ttr(dst[:, 0:P], s[:, 0:P], bt[:, n, 0:P], 1.0, 3e38, ALU.add, ALU.min, mn[:, 0, n:n + 1])
                signal(ttr(dst[:, P:SQ], s[:, P:SQ], bt[:, n, P:SQ], 1.0, 3e38, ALU.add, ALU.min, mn[:, 1, n:n + 1]), n_v)

            def weights_out(l, n):
                ve.wait_ge(pt_p, ALIBI * l + n + 1)
                if n >= 2:
                    ve.wait_ge(o_p, 13 * l + 1 + n - 1)
                signal(nc.vector.tensor_copy(pt[:, n % 2, :], bank[6 + n % 2][:, 0:SQ]), pt_c)

            def head_sums(m, o):
                own(o_v)
                then(tt(sq, o, o, ALU.mult))
                signal(nc.vector.tensor_reduce(st[:, 8:40].rearrange("p (b a) -> p b a", b=2)[:, :, m * NH:(m + 1) * NH],
                                               sq.rearrange("p b (a d) -> p b a d", d=HD), AX_X, ALU.add), hr_v)

            def mixer_out(l, s):
                m = SEQ[s]
                dst = xn[:, :, m * T:(m + 1) * T]
                ve.wait_ge(o_p, 13 * l + 1 + NH * s)
                if m == STICK:
                    signal(nc.vector.tensor_copy(dst, bank[3][:, :].rearrange("p (b n) -> p b n", b=2)), o_v)
                    head_sums(m, dst)
                    return
                hh = slice(NH * (s - 1), NH * s)
                then(nc.vector.reciprocal(rden[:, :, hh], den[:, :, hh]))
                signal(tt(dst.rearrange("p b (h d) -> p b h d", h=NH),
                          bank[3][:, :].rearrange("p (b h d) -> p b h d", b=2, h=NH),
                          rden[:, :, hh].unsqueeze(3).to_broadcast([P, 2, NH, HD]), ALU.mult), o_v)
                head_sums(m, dst)

            def index_sum(l, h):
                ve.wait_ge(is_a, IH * l + h + 1)
                if h:
                    own(is_v)
                elif l == 0:
                    ve.wait_ge(s_const2, 16)
                before = sc[:, 0, :] if h else ct[:, C_CAUSAL:C_CAUSAL + SQ]
                r = relu[:, h % 2, :]
                stt(sc[:, 0, 0:P], r[:, 0:P], iw[:, 0, h:h + 1], before[:, 0:P], ALU.mult, ALU.add)
                signal(stt(sc[:, 0, P:SQ], r[:, P:SQ], iw[:, 1, h:h + 1], before[:, P:SQ], ALU.mult, ALU.add), is_v)

            def top8(t):
                if t == 0:
                    own(is_v)
                a, b = sc[:, t % 2, :], sc[:, 1 - t % 2, :]
                for lo, hi in ((0, P), (P, SQ)):
                    then(nc.vector.max(v8, a[:, lo:hi]))
                    then(nc.vector.match_replace(b[:, lo:hi], v8, a[:, lo:hi], TAKEN))
                if t == TOPK_STEPS - 1:
                    then(ts(selm, sc[:, 0, :], TAKEN / 2, BIG, ALU.is_gt, ALU.mult))

            for l in range(DEPTH):
                if l == 0:
                    norm(0, 0)
                norm(2 * l, 1)
                turned(norm_no(l, 0))
                for what, n in PLANS[l]:
                    if what == "sum":
                        ada_take_all([ADA_ORDER[ADA_NO["ada", l, n] - 1]])
                        ada_sum(("ada", l, n), range(0, KC // 2))
                    elif what == "rest":
                        ada_sum(("ada", l, n), range(KC // 2, KC))
                    elif what == "is":
                        index_sum(l, n)
                    elif what == "z":
                        ve.wait_ge(z_p, NH * l + n + 1)
                        if n == 0:
                            own(is_v)
                        signal(tt(zb[:, n, :], bank[4 + n][:, 0:SQ], ct[:, C_STICK:C_STICK + SQ], ALU.add), z_v)
                    elif what == "topk":
                        top8(n)
                    elif what == "sp":
                        own(z_v)
                        ve.wait_ge(ze_a, 3 * l + 3)
                        for h in range(NH):
                            signal(stt(eb[:, h, :], zb[:, h, :], 0.0, eb[:, h, :], ALU.max, ALU.add), sp_r)
                    elif what == "suf":
                        own(sp_r)
                        ve.wait_ge(suf_p, NH * l + n + 1)
                        signal(tt(zb[:, n, :], zb[:, n, :], bank[4 + n][:, 0:SQ], ALU.add), stT_v)
                    elif what == "score":
                        biased(l, n)
                    elif what == "turn":
                        weights_out(l, n)
                    elif what == "out":
                        mixer_out(l, n)
                ada_take_all([("ada", 1, 11) if l else ("ada", 0, 9)])
                ve.wait_ge(hq_a, l + 1)
                then(nc.vector.reciprocal(st[:, 8:40], st[:, 8:40]))
                for m in range(MIX):
                    o = xn[:, :, m * T:(m + 1) * T].rearrange("p b (a d) -> p b a d", d=HD)
                    roots = st[:, 8:40].rearrange("p (b a) -> p b a", b=2)[:, :, m * NH:(m + 1) * NH]
                    signal(tt(o, o, roots.unsqueeze(3).to_broadcast([P, 2, NH, HD]), ALU.mult), on_v)
                turned(norm_no(l, 1))
                for n in range(4):
                    ve.wait_ge(wo_p, 4 * l + n + 1)
                    add_to_x(0, n % 2, n // 2, n)
                    if n == 2:
                        norm(2 * l + 1, 0)
                own(x_v)
                norm(2 * l + 1, 1)
                turned(norm_no(l, 2))
                if l == 0:
                    n = 0
                    for j in range(FJ):
                        if j >= 2:
                            ve.wait_ge(y_p, j - 1)
                        for t in range(ff_tiles(j)):
                            ve.wait_ge(sg_a, n + 1)
                            signal(tt(ffT[:, j % 2, t, :], fsg[:, n % 2, :], bank[n % 2][:, T:2 * T], ALU.mult), h_v)
                            n += 1
                            if t % 2 == 0:
                                ada(ada_after(l, ("ffu", 0, j))[t // 2:t // 2 + 1], wait=False)
                    ada_take_all([("ada", 1, 8)])
                    for n in range(4):
                        ve.wait_ge(y_p, FJ + n)
                        add_to_x(1, n % 2, n // 2, n)
                        if n == 2:
                            norm(2, 0)
                    own(x_v)

            ve.wait_ge(r_p, 1)
            then(nc.vector.tensor_copy(lg, bank[0][:, 0:2 * NE].rearrange("p (b e) -> p b e", b=2)))
            for b in range(2):
                then(nc.vector.max(top[:, b, :], lg[:, b, :]))
                then(nc.vector.max_index(topi[:, b, :], top[:, b, :], lg[:, b, :]))
            then(nc.vector.tensor_copy(topf, topi[:, :, :]))
            for b in range(2):
                for k in range(2):
                    then(ts(oh[:, b, k, :], ct[:, C_IOTA:C_IOTA + NE], topf[:, b, k:k + 1], None, ALU.is_equal))
            signal(tt(chosen, oh[:, :, 0, :], oh[:, :, 1, :], ALU.add), sel_v)
            signal(tt(gt[:, :, 0], top[:, :, 1], top[:, :, 0], ALU.subtract), r_v)
            ve.wait_ge(r_a, 1)
            then(ts(gt[:, :, 2], gt[:, :, 1], 1.0, None, ALU.add))
            then(nc.vector.reciprocal(gt[:, :, 2], gt[:, :, 2]))
            then(tt(gt[:, :, 3], gt[:, :, 1], gt[:, :, 2], ALU.mult))
            own(sel_v)
            for b in range(2):
                then(ts(gate[:, b, 0:NE], oh[:, b, 0, :], gt[:, b, 2:3], None, ALU.mult))
                then(stt(gate[:, b, 0:NE], oh[:, b, 1, :], gt[:, b, 3:4], gate[:, b, 0:NE], ALU.mult, ALU.add))
            ve.wait_ge(r_p, 2)
            then(tt(pos[:, :, 0:NE], bank[1][:, 0:2 * NE].rearrange("p (b e) -> p b e", b=2), chosen, ALU.mult))
            then(ts(nblk, bank[1][:, 2 * NE:3 * NE], float(BT), 1.0, ALU.is_gt, ALU.add))
            for q in range(2, NB):
                then(stt(nblk, bank[1][:, 2 * NE:3 * NE], float(q * BT), nblk, ALU.is_gt, ALU.add))
            signal(nc.vector.memset(pos[:, :, NE:NE + 1], 0.0), dv)
            signal(nc.vector.memset(gate[:, :, NE:NE + 1], 0.0), dv)
            own(dv)
            signal(nc.vector.memset(route[:, 0, 0:1], 0.0), dv)
            then(nc.vector.tensor_copy(route[:, 1, 0:1], nblk[:, 0:1]))
            signal(nc.vector.tensor_copy(route_i[:, :, 0:1], route[:, :, 0:1]), route_v)
            own(route_v)

            def one_hots(r):
                e = expert_of(ve, r, NE)
                slots = ct[:, C_SLOT:C_SLOT + T]
                for b in range(2):
                    p_, g_ = pos[:, b, bass.ds(e, 1)], gate[:, b, bass.ds(e, 1)]
                    ts(sel01[:, b, :], slots, p_, None, ALU.is_equal)
                    for c2 in range(2):
                        ts(selg[:, b, 0:2, c2 * BT:(c2 + 1) * BT], slots.rearrange("p (q n) -> p q n", q=2)[:, :, 0:BT],
                           p_, g_, ALU.is_equal, ALU.mult)
                    last = ts(selg[:, b, 2:4, :].rearrange("p q n -> p (q n)"), slots, p_, g_, ALU.is_equal, ALU.mult)
                last.then_inc(sel_v, 1)

            def expert(r, nb):
                base = r * (NB * EJ)
                ve.wait_ge(gat_p, r + 1)
                for k in range(KC // 2):
                    ts(xsT[:, k, 0:nb * BT], bank[4 + k // 2][:, (k % 2) * T:(k % 2) * T + nb * BT],
                       acol[:, 1, 1, k:k + 1], mcol[:, 1, 24 + k:25 + k], ALU.mult, ALU.add).then_inc(xsT_v, 1)
                ve.wait_ge(sgt_p, r + 1)
                for n in range(len(UNITS[nb])):
                    last = nc.vector.tensor_copy(selgT[:, n, :], bank[2 + n][:, 0:T])
                last.then_inc(sgt_v, 1)
                seq = [(j, q) for j in range(EJ) for q in range(nb)]
                for i, (j, q) in enumerate(seq):
                    ve.wait_ge(esg_a, base + value(nb, j, q))
                    if i >= 2:
                        ve.wait_ge(et_p, base + value(nb, *seq[i - 2]))
                    tt(hs[:, i % 2, :], sg[:, i % 2, :], bank[i % 2][:, HC:2 * HC], ALU.mult)\
                        .then_inc(eh_v, steps(nb, q))

            one_hots(0)
            signal(nc.vector.memset(yacc, 0.0), yacc_v)
            signal(nc.vector.memset(route[:, 0, NE:NE + 1], float(NE)), dv)
            signal(nc.vector.memset(route[:, 1, NE:NE + 1], 1.0), dv)
            then(stt(rank[:, 0, :], nblk, float(2 * NE), ct[:, C_IOTA:C_IOTA + NE], ALU.mult, ALU.subtract))
            then(ts(rank[:, 0, 0:1], rank[:, 0, 0:1], float(2 * NE * NB), None, ALU.add))
            then(nc.vector.max(rank[:, 1, :], rank[:, 0, :]))
            then(nc.vector.max_index(topi[:, 0, :], rank[:, 1, :], rank[:, 0, :]))
            then(nc.vector.tensor_copy(rank[:, 0, :], topi[:, 0, :]))
            then(tt(rank[:, 1, :], rank[:, 1, :], rank[:, 0, :], ALU.add))
            then(ts(rank[:, 1, :], rank[:, 1, :], 1.0 / (2 * NE), None, ALU.mult))
            then(ts(rank[:, 1, 0:1], rank[:, 1, 0:1], -float(NB), None, ALU.add))
            for to, fro in list(enumerate(TURNS))[1:]:
                signal(nc.vector.tensor_copy(route[:, :, to:to + 1], rank[:, :, fro:fro + 1]), dv)
            own(dv)
            signal(nc.vector.tensor_copy(route_i[:, :, 1:], route[:, :, 1:]), route_v)
            own(route_v)
            with ve.Fori(0, NE) as r:
                blocks = blocks_of(ve, r)
                for nb in range(1, NB + 1):
                    with ve.If(blocks == nb):
                        expert(r, nb)
                one_hots(r + 1)
                ve.wait_ge(sct_p, r + 1)
                ve.wait_ge(yacc_v, 4 * r + 1)
                for b in range(2):
                    for hf in range(2):
                        y_ = yacc[:, b, hf * CW:(hf + 1) * CW]
                        tt(y_, y_, bank[2 * hf + b][:, :], ALU.add).then_inc(yacc_v, 1)
            ve.wait_ge(yacc_v, 4 * NE + 1)
            for b in range(2):
                then(tt(yacc[:, b, :], yacc[:, b, :], gates[:, 1, :], ALU.mult))
                signal(tt(xs[:, b, :], xs[:, b, :], yacc[:, b, :], ALU.add), x_v)
            own(x_v)
            ve.wait_ge(s_gfin, 16)
            for b in range(2):
                ve.wait_ge(sq_r, 9 + b)
                then(nc.vector.reciprocal(st[:, 4 + b:5 + b], st[:, 2 + b:3 + b]))
                stt(xn[:, b, :], xs[:, b, :], st[:, 4 + b:5 + b], gfin, ALU.mult, ALU.mult).then_inc(fin_v, 1)

        @block.scalar
        def _(ae):
            act = nc.scalar.activation
            eps, one = epst[:, 0:1], epst[:, 1:2]

            def norm(no, x_ready):
                if no in (2, 4):
                    act(st[:, 5 + no // 2:6 + no // 2], epst[:, 1:2], ACT.Sqrt)
                for b in range(2):
                    x_ready(b)
                    act(xn[:, b, :], xs[:, b, :], ACT.Square, accum_out=st[:, b:b + 1]).then_inc(ss_r, 1)
                    ae.wait_ge(ss_r, 2 * no + b + 1)
                    act(st[:, 2 + b:3 + b], st[:, b:b + 1], ACT.Sqrt, bias=eps, scale=1.0 / D).then_inc(sq_r, 1)

            def turned(no, scales):
                l, which = no // 3, no % 3
                ae.wait_ge(ada_c, ADA_NO[scales] + 1)
                for k in (2, 3, 6, 7):
                    g = k // 2
                    ae.wait_ge(tr_p, 4 * no + g + 1)
                    src = bank[4 + g][:, (k % 2) * T:(k % 2 + 1) * T]
                    if which == 1:
                        ins = act(hT[:, k, :], src, ACT.Copy, scale=cols[:, 128 + 8 * l + k:129 + 8 * l + k])
                    else:
                        w = which // 2
                        ins = act(hT[:, k, :], src, ACT.Identity, scale=acol[:, l, w, k:k + 1],
                                  bias=mcol[:, l, 24 * w + k:24 * w + k + 1])
                    ins.then_inc(tr_a, 1)

            def copied(l, g):
                G = 25 * l + g
                o = bank[G % 2]
                ae.wait_ge(proj_p, G + 1)
                if g < 4:
                    ins = act(iq[:, g, :], o[:, 0:T], ACT.Copy)
                elif g == 4:
                    act(ik, o[:, 0:T], ACT.Copy)
                    ins = act(iw.rearrange("p b h -> p (b h)"), o[:, T:T + 2 * IH], ACT.Copy,
                              scale=float(HD ** -0.5 * IH ** -0.5))
                else:
                    s, t = divmod(g - 5, 5)
                    if t == 4:
                        ins = act(vAB[:, s] if s < 2 else vCD[:, s - 2], o[:, :].rearrange("p (b n) -> p b n", b=2), ACT.Copy)
                    else:
                        ins = act(qkT[:, s % 2, t, :], o[:, 0:T], ACT.Copy,
                                  scale=1.0 if t >= 2 else (-0.125 if s else 0.125))
                ins.then_inc(proj_c, 1)

            def exps(l, n):
                N = ALIBI * l + n
                ae.wait_ge(n_v, N + 1)
                if n >= 2:
                    ae.wait_ge(pt_p, N - 1)
                act(ex[:, n % 2, 0:P], neg[:, n % 2, 0:P], ACT.Exp, bias=mn[:, 0, n:n + 1], scale=-1.0,
                    accum_out=den[:, 0, n:n + 1])
                act(ex[:, n % 2, P:SQ], neg[:, n % 2, P:SQ], ACT.Exp, bias=mn[:, 1, n:n + 1], scale=-1.0,
                    accum_out=den[:, 1, n:n + 1]).then_inc(e_a, 1)

            ae.wait_ge(setup_c, 1)
            act(cond[:, :], cols[:, 144:152], ACT.Silu).then_inc(cond_r, 1)
            for l in range(DEPTH):
                norm(2 * l, (lambda b: ae.wait_ge(x_v, 6 + 2 * b)) if l else (lambda b: ae.wait_ge(s_x, 16)))
                turned(norm_no(l, 0), ("ada", l, 3))
                for what, n in PLANS[l]:
                    if what == "proj":
                        copied(l, n)
                    elif what == "is":
                        ae.wait_ge(is_p, IH * l + n + 1)
                        if n >= 2:
                            ae.wait_ge(is_v, IH * l + n - 1)
                        act(relu[:, n % 2, :], bank[4 + n % 4][:, 0:SQ], ACT.Relu).then_inc(is_a, 1)
                    elif what == "ln":
                        ae.wait_ge(z_v, NH * (l + 1))
                        act(eb[:, :, :], zb[:, :, :], ACT.Abs).then_inc(ze_a, 1)
                        ae.wait_ge(ze_a, 3 * l + 1)
                        act(eb[:, :, :], eb[:, :, :], ACT.Exp, scale=-1.0).then_inc(ze_a, 1)
                        ae.wait_ge(ze_a, 3 * l + 2)
                        act(eb[:, :, :], eb[:, :, :], ACT.Ln, bias=one).then_inc(ze_a, 1)
                    elif what == "suf":
                        ae.wait_ge(stT_v, NH * l + n + 1)
                        act(zb[:, n, :], zb[:, n, :], ACT.Exp).then_inc(stA_a, 1)
                    elif what == "score":
                        exps(l, n)
                ae.wait_ge(hr_v, MIX * (l + 1))
                act(st[:, 8:40], st[:, 8:40], ACT.Sqrt, bias=eps, scale=1.0 / HD).then_inc(hq_a, 1)
                turned(norm_no(l, 1), ("ada", l, 9))
                norm(2 * l + 1, lambda b: ae.wait_ge(x_v, 8 * l + 2 + 2 * b))
                if l:
                    ae.dma_start(wr, w_router[0].rearrange("(c p) e -> p c e", p=P)).then_inc(s_wr, 16)
                turned(norm_no(l, 2), ("ada", l, 9))
                if l == 0:
                    for n in range(FF // P):
                        ae.wait_ge(gu_p, n + 1)
                        if n >= 2:
                            ae.wait_ge(h_v, n - 1)
                        act(fsg[:, n % 2, :], bank[n % 2][:, 0:T], ACT.Silu).then_inc(sg_a, 1)
            ae.wait_ge(r_v, 1)
            act(gt[:, :, 1], gt[:, :, 0], ACT.Exp).then_inc(r_a, 1)
            ae.wait_ge(route_v, 1)

            def expert(r, nb):
                base = r * (NB * EJ)
                ae.wait_ge(gat_p, r + 1)
                for k in range(KC // 2, KC):
                    act(xsT[:, k, 0:nb * BT], bank[4 + k // 2][:, (k % 2) * T:(k % 2) * T + nb * BT], ACT.Identity,
                        scale=acol[:, 1, 1, k:k + 1], bias=mcol[:, 1, 24 + k:25 + k]).then_inc(xsT_a, 1)
                seq = [(j, q) for j in range(EJ) for q in range(nb)]
                for i in range(len(seq) + 1):
                    if i:
                        ae.wait_ge(et_p, base + value(nb, *seq[i - 1]))
                        if i >= 3:
                            ae.wait_ge(ey_p, base + value(nb, *seq[i - 3]))
                        act(hsT[:, (i - 1) % 2, :, :],
                            bank[2 + (i - 1) % 2][:, 0:HC].rearrange("p (t n) -> p t n", t=2), ACT.Copy)\
                            .then_inc(et_a, steps(nb, seq[i - 1][1]))
                    if i < len(seq):
                        ae.wait_ge(egu_p, base + value(nb, *seq[i]))
                        if i >= 2:
                            ae.wait_ge(eh_v, base + value(nb, *seq[i - 2]))
                        act(sg[:, i % 2, :], bank[i % 2][:, 0:HC], ACT.Silu).then_inc(esg_a, steps(nb, seq[i][1]))
                ae.wait_ge(ey_p, base + NB * EJ)
                for q in range(nb):
                    last = act(ys[:, q, :], bank[4 + q][:, :], ACT.Copy)
                last.then_inc(ys_a, 1)

            with ae.Fori(0, NE) as r:
                blocks = blocks_of(ae, r)
                for nb in range(1, NB + 1):
                    with ae.If(blocks == nb):
                        expert(r, nb)
            norm(4, lambda b: ae.wait_ge(x_v, 13 + b))


def kernel(**inputs):
    import concourse.bacc as bacc
    from concourse.bass_utils import run_bass_kernel_spmd

    names = ["x", "c", "w_ada", "b_ada", "g_mix", "w_in", "g_heads", "w_out", "g_ffn", "w_ff_gate", "w_ff_up",
             "w_ff_down", "w_router", "w_exp_gate", "w_exp_up", "w_exp_down", "g_final"]
    nc = bacc.Bacc("TRN2", target_bir_lowering=False, num_devices=1)
    arrays = {f"in_{n}": np.ascontiguousarray(inputs[n]) for n in names}
    arrays["ctab"], arrays["btab"] = constants()
    args = [nc.dram_tensor(n, a.shape, F32, kind="ExternalInput").ap() for n, a in arrays.items()]
    args.append(nc.dram_tensor("out", (1, T, D), F32, kind="ExternalOutput").ap())
    build(nc, *args)
    r = run_bass_kernel_spmd(nc, [arrays], core_ids=[0])
    return r.results[0]["out"]
```
